# Optimizing a Trainium2 kernel written in Bass

```python
import math
import jax
import jax.numpy as jnp
from jax import lax
import numpy as np

D_MODEL = 2048
BATCH = 1
SEQ = 256
DEPTH = 1

MIX_WIDTH = D_MODEL
ATTN_WIDTH = MIX_WIDTH // 2
ATTN_HEAD_DIM = 128
N_ATTN_HEADS = ATTN_WIDTH // ATTN_HEAD_DIM
RET_WIDTH = MIX_WIDTH - ATTN_WIDTH
RET_HEAD_DIM = 256
N_RET_HEADS = RET_WIDTH // RET_HEAD_DIM
RET_CHUNK = 128
DILATED_PATTERNS = ((128, 1), (512, 4), (2048, 16))
FFN_HIDDEN = ((8 * D_MODEL // 3 + 255) // 256) * 256
IN_PROJ_WIDTH = 3 * ATTN_WIDTH + 4 * RET_WIDTH
NORM_EPS = 1e-6

kernel_name = "hybrid_dilated_attn_retention_block"

def _rmsnorm(x, w):
    x32 = x.astype(jnp.float32)
    y = x32 * lax.rsqrt(jnp.mean(x32 * x32, axis=-1, keepdims=True) + NORM_EPS)
    return (y * w.astype(jnp.float32)).astype(x.dtype)

def _alibi_slopes(n_heads):
    return jnp.exp2(-8.0 * jnp.arange(1, n_heads + 1, dtype=jnp.float32) / n_heads)

def _dilated_branch(q, k, v, slopes, window, dilation):
    B, H, S, hd = q.shape
    blk = window // dilation
    span = dilation * blk
    sp = -(-S // span) * span
    L = sp // dilation
    nb = L // blk

    def to_sub(t):
        t = jnp.pad(t, ((0, 0), (0, 0), (0, sp - S), (0, 0)))
        t = t.reshape(B, H, L, dilation, hd).transpose(0, 1, 3, 2, 4)
        return t.reshape(B, H, dilation, nb, blk, hd)

    def two_block(t):
        prev = jnp.concatenate([jnp.zeros_like(t[:, :, :, :1]), t[:, :, :, :-1]], axis=3)
        return jnp.concatenate([prev, t], axis=4)

    qb = to_sub(q)
    kk = two_block(to_sub(k))
    vv = two_block(to_sub(v))
    s = jnp.einsum('bhrnqd,bhrnkd->bhrnqk', qb, kk).astype(jnp.float32) * (1.0 / math.sqrt(hd))
    qi = jnp.arange(blk)[:, None]
    kj = jnp.arange(2 * blk)[None, :]
    diff = qi - kj + blk
    key_idx = jnp.arange(nb)[:, None, None] * blk + kj[None] - blk
    valid = (diff >= 0) & (diff <= blk) & (key_idx >= 0)
    bias = -slopes[:, None, None] * (diff * dilation).astype(jnp.float32)
    s = s + bias[None, :, None, None]
    s = jnp.where(valid, s, -jnp.inf)
    lse = jax.nn.logsumexp(s, axis=-1)
    p = jnp.exp(s - lse[..., None])
    o = jnp.einsum('bhrnqk,bhrnkd->bhrnqd', p.astype(v.dtype), vv)

    def from_sub(t):
        tail = t.shape[5:]
        t = t.reshape((B, H, dilation, L) + tail)
        t = jnp.moveaxis(t, 2, 3)
        return t.reshape((B, H, sp) + tail)[:, :, :S]

    return from_sub(o), from_sub(lse)

def _dilated_attention(q, k, v):
    slopes = _alibi_slopes(q.shape[1])
    outs, lses = [], []
    for window, dilation in DILATED_PATTERNS:
        o, l = _dilated_branch(q, k, v, slopes, window, dilation)
        outs.append(o.astype(jnp.float32))
        lses.append(l)
    wts = jax.nn.softmax(jnp.stack(lses), axis=0)
    return jnp.sum(wts[..., None] * jnp.stack(outs), axis=0)

def _retention_chunkwise(q, k, v):
    B, H, S, dh = q.shape
    C = RET_CHUNK
    nc = S // C
    log_gamma = jnp.log(1.0 - jnp.exp2(-5.0 - jnp.arange(H, dtype=jnp.float32)))
    k = k * (1.0 / math.sqrt(dh))
    qc = q.reshape(B, H, nc, C, dh)
    kc = k.reshape(B, H, nc, C, dh)
    vc = v.reshape(B, H, nc, C, dh)
    idx = jnp.arange(C, dtype=jnp.float32)
    dif = idx[:, None] - idx[None, :]
    decay = jnp.where(dif >= 0, jnp.exp(log_gamma[:, None, None] * jnp.maximum(dif, 0.0)), 0.0)
    scores = jnp.einsum('bhnid,bhnjd->bhnij', qc, kc) * decay[None, :, None]
    inner = jnp.einsum('bhnij,bhnjd->bhnid', scores, vc)
    zeta = jnp.exp(log_gamma[:, None] * (C - 1.0 - idx))
    kv = jnp.einsum('bhnjd,bhnje->bhnde', kc * zeta[None, :, None, :, None], vc)
    gamma_chunk = jnp.exp(log_gamma * C)[None, :, None, None]

    def step(state, kv_n):
        return state * gamma_chunk + kv_n, state

    _, r_prev = lax.scan(step, jnp.zeros((B, H, dh, dh), jnp.float32), jnp.moveaxis(kv, 2, 0))
    r_prev = jnp.moveaxis(r_prev, 0, 2)
    xi = jnp.exp(log_gamma[:, None] * (idx + 1.0))
    cross = jnp.einsum('bhnid,bhnde->bhnie', qc, r_prev) * xi[None, :, None, :, None]
    return (inner + cross).reshape(B, H, S, dh)

def _heads(t, n_heads, head_dim):
    B, S, _ = t.shape
    return t.reshape(B, S, n_heads, head_dim).transpose(0, 2, 1, 3)

def _merge(t):
    B, H, S, hd = t.shape
    return t.transpose(0, 2, 1, 3).reshape(B, S, H * hd)

def _hybrid_mixer(h, w_in, w_out):
    proj = jnp.einsum('bsd,de->bse', h, w_in)
    cuts = np.cumsum([ATTN_WIDTH] * 3 + [RET_WIDTH] * 3)
    qa, ka, va, qr, kr, vr, gr = jnp.split(proj, cuts, axis=-1)
    attn = _dilated_attention(_heads(qa, N_ATTN_HEADS, ATTN_HEAD_DIM),
                              _heads(ka, N_ATTN_HEADS, ATTN_HEAD_DIM),
                              _heads(va, N_ATTN_HEADS, ATTN_HEAD_DIM))
    f32 = jnp.float32
    ret = _retention_chunkwise(_heads(qr, N_RET_HEADS, RET_HEAD_DIM).astype(f32),
                               _heads(kr, N_RET_HEADS, RET_HEAD_DIM).astype(f32),
                               _heads(vr, N_RET_HEADS, RET_HEAD_DIM).astype(f32))
    ret = ret * lax.rsqrt(jnp.mean(ret * ret, axis=-1, keepdims=True) + NORM_EPS)
    ret = jax.nn.silu(gr.astype(f32)) * _merge(ret)
    mixed = jnp.concatenate([_merge(attn), ret], axis=-1).astype(h.dtype)
    return jnp.einsum('bse,ed->bsd', mixed, w_out)

def _swiglu(h, w_gate, w_up, w_down):
    g = jnp.einsum('bsd,df->bsf', h, w_gate)
    u = jnp.einsum('bsd,df->bsf', h, w_up)
    return jnp.einsum('bsf,fd->bsd', jax.nn.silu(g) * u, w_down)

def setup_inputs(seed: int = 0) -> dict:
    key = jax.random.key(seed)
    ks = jax.random.split(key, 10)
    f32 = jnp.float32

    def normal(k, shape, fan_in):
        return jax.random.normal(k, shape, f32) * (fan_in ** -0.5)

    return {
        "x": jax.random.normal(ks[0], (BATCH, SEQ, D_MODEL), f32),
        "norm_mix_w": 1.0 + 0.02 * jax.random.normal(ks[1], (DEPTH, D_MODEL), f32),
        "w_in": normal(ks[2], (DEPTH, D_MODEL, IN_PROJ_WIDTH), D_MODEL),
        "w_out": normal(ks[3], (DEPTH, MIX_WIDTH, D_MODEL), MIX_WIDTH),
        "norm_ffn_w": 1.0 + 0.02 * jax.random.normal(ks[4], (DEPTH, D_MODEL), f32),
        "w_gate": normal(ks[5], (DEPTH, D_MODEL, FFN_HIDDEN), D_MODEL),
        "w_up": normal(ks[6], (DEPTH, D_MODEL, FFN_HIDDEN), D_MODEL),
        "w_down": normal(ks[7], (DEPTH, FFN_HIDDEN, D_MODEL), FFN_HIDDEN),
        "norm_final_w": 1.0 + 0.02 * jax.random.normal(ks[8], (D_MODEL,), f32),
    }

def reference(x, norm_mix_w, w_in, w_out, norm_ffn_w, w_gate, w_up, w_down, norm_final_w):
    for layer in range(DEPTH):
        h = _rmsnorm(x, norm_mix_w[layer])
        x = x + _hybrid_mixer(h, w_in[layer], w_out[layer])
        h = _rmsnorm(x, norm_ffn_w[layer])
        x = x + _swiglu(h, w_gate[layer], w_up[layer], w_down[layer])
    return _rmsnorm(x, norm_final_w)


_drawn_inputs = setup_inputs


def setup_inputs(seed=0):
    import zlib

    import numpy as np

    out = dict(_drawn_inputs(seed))
    spreads = {}
    factors = {'norm_mix_w': 2.897, 'norm_ffn_w': 4.223, 'norm_final_w': 2.859}
    for name, (base, spread) in spreads.items():
        noise = np.random.default_rng([zlib.crc32(name.encode()), seed]).standard_normal(out[name].shape)
        drawn = base * np.exp(spread * noise) if base else spread * noise
        out[name] = jnp.asarray(drawn.astype(out[name].dtype))
    for name, factor in factors.items():
        out[name] = (out[name] * factor).astype(out[name].dtype)
    return out
```

```python
import concourse.bass as bass
from concourse import mybir
from contextlib import ExitStack

F32 = mybir.dt.float32
F32R = mybir.dt.float32r
ALU = mybir.AluOpType
ACT = mybir.ActivationFunctionType
AX_X = mybir.AxisListType.X

P = 128
T = 256
HALVES = T // P
D = 2048
NB = 512
KT = D // P
F = 5632
FKT = F // P
A_HEADS, A_DIM = 8, 128
R_HEADS, R_DIM = 4, 256
MIX = 1024
EPS = 1e-6
SQ = 384

RAW = 4
RING = 4
AHEAD = 4

IN_BLOCKS, OUT_BLOCKS, FFN_STEPS, DOWN_BLOCKS = 14, D // NB, F // NB, D // NB
PAIRS = KT // 2
DPAIRS = FKT // 2
CHUNKS, DCHUNKS = PAIRS // 2, DPAIRS // 2
OUT0 = IN_BLOCKS
FFN0 = OUT0 + OUT_BLOCKS
DOWN0 = FFN0 + 2 * FFN_STEPS

QA, KA, VA, QR, KR, VR, GR = range(7)
IN_ORDER = [(s, n) for s in (QA, KA, VA, VR, KR, QR, GR) for n in range(2)]


CONSTS = 6
ATTN_AT = 41
RET_AT = (96, 98, 104, 106)

TB_IN = {b: 4 + i for i, b in enumerate(b for b, (s, _) in enumerate(IN_ORDER) if s in (QA, KA, KR, QR))}
TB_GATED = [4 + len(TB_IN), 5 + len(TB_IN)]
TB_X2 = TB_GATED[1] + 1
TB_H = TB_X2 + 4


def hi_banks(batch):
    return batch * 2 if isinstance(batch, int) and batch < 4 else batch * 2 - 2 * len(TB_IN)


def slot_uses(slot):
    return len(range(slot, DCHUNKS, RAW))


class Plan:

    def __init__(self):
        self.after = {}

    def put(self, blk, pair, work):
        self.after.setdefault(PAIRS * blk + pair, []).append(work)

    def of(self, blk):
        return {j: self.after[PAIRS * blk + j] for j in range(PAIRS) if PAIRS * blk + j in self.after}


def slot_last_user(j, slots, per_block, first_block):
    if j >= slots or first_block or per_block % slots == 0:
        return slots
    last = max(k for k in range(per_block) if k % slots == j)
    return per_block + j - last


def build(nc, x, norm_mix_w, w_in, w_out, norm_ffn_w, w_gate, w_up, w_down, norm_final_w,
          ident_c, dist_c, count_c, decay_c, out, slopes):
    base = -(-nc.sbuf_base // 64) * 64

    def place(name, shape, dt, offset):
        return nc.alloc_sbuf_tensor_at(name, shape, dt, offset=base + offset)

    KB = 1024
    xT_hi = place("xT_hi", [P, KT, T], F32R, 0)
    xT_lo = place("xT_lo", [P, KT, T], F32R, 16 * KB)
    wfin = place("wfin", [P, D], F32, 0)
    xres = place("xres", [P, HALVES, D], F32, 32 * KB)
    region = 48 * KB
    hT_hi = place("hT_hi", [P, FKT, T], F32R, region)
    hT_lo = place("hT_lo", [P, FKT, T], F32R, region + 44 * KB)
    mixT_hi = place("mixT_hi", [P, KT, T], F32R, region)
    mixT_lo = place("mixT_lo", [P, KT, T], F32R, region + 16 * KB)
    qT = place("qT", [P, MIX // P, T], F32, region + 32 * KB)
    kT = place("kT", [P, MIX // P, T], F32, region + 40 * KB)
    va = place("va", [P, HALVES, MIX], F32, region + 48 * KB)
    retn = place("retn", [P, HALVES, MIX], F32, region + 48 * KB)
    vr = place("vr", [P, HALVES, MIX], F32, region + 56 * KB)
    sgr = place("sgr", [P, HALVES, MIX], F32, region + 64 * KB)
    dist = place("dist", [P, SQ], F32, region + 72 * KB)
    count = place("count", [P, SQ], F32, region + 72 * KB + 1536)
    decay = place("decay", [P, R_HEADS, SQ], F32, region + 75 * KB)
    probs = place("probs", [P, 2, SQ], F32, region + 81 * KB)
    pT = place("pT", [P, 2, SQ], F32, region + 84 * KB)
    raw = place("raw", [P, RAW, 4, NB], F32, 136 * KB)
    w_hi = place("w_hi", [P, RING, 2, NB], F32R, 168 * KB)
    w_lo = place("w_lo", [P, RING, 2, NB], F32R, 184 * KB)
    stage = place("stage", [P, HALVES, NB], F32, 200 * KB)
    small_at = [204 * KB]

    def small(name, shape, dt=F32):
        n = 4
        for d in shape[1:]:
            n *= d
        offset = small_at[0]
        small_at[0] += -(-n // 32) * 32
        return place(name, shape, dt, offset)

    wrow = place("wrow", [KT, P], F32, 204 * KB)
    wrow2 = place("wrow2", [KT, P], F32, 204 * KB + 512)
    junk = small("junk", [P, NB])
    ident = small("ident", [P, P])
    wcol = small("wcol", [P, KT])
    wcol2 = small("wcol2", [P, KT])
    sumsq = small("sumsq", [P, 3, HALVES, 4])
    tot = small("tot", [P, 3, HALVES])
    meansq = small("meansq", [P, 3, HALVES])
    rstd = small("rstd", [P, 3, HALVES])
    rstd_q = small("rstd_q", [P, HALVES])
    mhalf = small("mhalf", [P, HALVES])
    rowmax = small("rowmax", [P, 2, HALVES])
    negmax = small("negmax", [P, 2, HALVES])
    den = small("den", [P, 2, HALVES])
    rden = small("rden", [P, 2, HALVES])
    rsum = small("rsum", [P, R_HEADS, HALVES])
    rmean = small("rmean", [P, R_HEADS, HALVES])
    rrstd = small("rrstd", [P, R_HEADS, HALVES])

    x_d = x.rearrange("b (h p) d -> (b p) h d", p=P)
    out_d = out.rearrange("b (h p) d -> (b p) h d", p=P)
    w_in_d = w_in.rearrange("l (k p) n -> (l p) k n", p=P)
    w_out_d = w_out.rearrange("l (k p) n -> (l p) k n", p=P)
    w_gate_d = w_gate.rearrange("l (k p) n -> (l p) k n", p=P)
    w_up_d = w_up.rearrange("l (k p) n -> (l p) k n", p=P)
    w_down_d = w_down.rearrange("l (k p) n -> (l p) k n", p=P)

    with ExitStack() as ctx:
        def sem(name):
            return ctx.enter_context(nc.semaphore(name))

        def bank(name, shape):
            return ctx.enter_context(nc.psum_tensor(name, shape, F32))

        acc = bank("acc", [P, 2, HALVES, NB])
        tp = bank("tp", [P, 2, 2, T])
        sc = bank("sc", [P, NB])
        ot = bank("ot", [P, NB])

        const_in = sem("const_in")
        x_in = [sem(f"x_in{q}") for q in range(4)]
        wfin_in = sem("wfin_in")
        raw_in = [sem(f"raw_in{s}") for s in range(RAW)]
        hi_ready = sem("hi_ready")
        lo_ready = sem("lo_ready")
        pair_used = sem("pair_used")
        acc_read = [sem(f"acc_read{h}") for h in range(HALVES)]
        tp_full = sem("tp_full")
        tp_hi = sem("tp_hi")
        tp_free = sem("tp_free")
        wcol_full = sem("wcol_full")
        wcol_ready = sem("wcol_ready")
        mhalf_ready = sem("mhalf_ready")
        sq_done = sem("sq_done")
        tot_done = sem("tot_done")
        mean_done = sem("mean_done")
        rstd_done = sem("rstd_done")
        rstd_q_done = sem("rstd_q_done")
        sc_full = sem("sc_full")
        sc_free = sem("sc_free")
        max_done = sem("max_done")
        neg_done = sem("neg_done")
        exp_done = sem("exp_done")
        den_done = sem("den_done")
        rden_done = sem("rden_done")
        p_ready = sem("p_ready")
        pT_full = sem("pT_full")
        pT_ready = sem("pT_ready")
        ot_full = sem("ot_full")
        ot_hi = sem("ot_hi")
        ot_free = sem("ot_free")
        ret_sq = sem("ret_sq")
        ret_mean = sem("ret_mean")
        ret_rstd = sem("ret_rstd")
        gated = sem("gated")
        z_done = sem("z_done")
        y_act = sem("y_act")
        y_dve = sem("y_dve")
        out_done = sem("out_done")

        tp_flat = tp[:, 0, :, :].rearrange("p a b -> p (a b)")
        block = ctx.enter_context(nc.Block())

        @block.sync
        def _(sp):
            for q in range(4):
                sp.dma_start(xres[:, :, NB * q:NB * (q + 1)], x_d[:, :, NB * q:NB * (q + 1)]).then_inc(x_in[q], 16)

            def load_block(w, col, blk):
                for c in range(CHUNKS):
                    if not isinstance(blk, int) or blk > 0:
                        sp.wait_ge(lo_ready, blk * PAIRS + (2 * c + 2 - PAIRS))
                    sp.dma_start(raw[:, c, :, :], w[:, 4 * c:4 * c + 4, bass.ds(col, NB)]).then_inc(raw_in[c], 16)

            for b, (s, n) in enumerate(IN_ORDER):
                load_block(w_in_d, MIX * s + NB * n, b)
            for n in range(OUT_BLOCKS):
                load_block(w_out_d, NB * n, OUT0 + n)
            with sp.Fori(0, FFN_STEPS) as i:
                load_block(w_gate_d, i * NB, i * 2 + FFN0)
                load_block(w_up_d, i * NB, i * 2 + (FFN0 + 1))

            def load_down(n):
                for c in range(DCHUNKS):
                    back = slot_last_user(c, RAW, DCHUNKS, isinstance(n, int) and n == 0)
                    sp.wait_ge(lo_ready, n * DPAIRS + (PAIRS * DOWN0 + 2 * (c - back) + 2))
                    sp.dma_start(raw[:, c % RAW, :, :],
                                 w_down_d[:, 4 * c:4 * c + 4, bass.ds(n * NB, NB)]).then_inc(raw_in[c % RAW], 16)

            load_down(0)
            sp.wait_ge(pair_used, PAIRS * DOWN0)
            sp.dma_start(wfin[:, :], norm_final_w.partition_broadcast(P)).then_inc(wfin_in, 16)
            with sp.Fori(1, DOWN_BLOCKS) as n:
                load_down(n)
            for h in range(HALVES):
                for c, done in enumerate((y_act, y_dve)):
                    sp.wait_ge(done, h + 1)
                    sp.dma_start(out_d[:, h, (D // 2) * c:(D // 2) * (c + 1)],
                                 xres[:, h, (D // 2) * c:(D // 2) * (c + 1)]).then_inc(out_done, 16)
            sp.wait_ge(out_done, 16 * 2 * HALVES)

        @block.tensor
        def _(pe):
            def multiply_block(a_hi, a_lo, pairs, before, blk, parity, hooks, inputs=None):
                first = isinstance(before, int) and before <= PAIRS * DOWN0
                if not isinstance(blk, int) or blk >= 2:
                    for h in range(HALVES):
                        pe.wait_ge(acc_read[h], blk - 1)
                for j in range(pairs):
                    for wait in (inputs or {}).get(j, ()):
                        wait()
                    pe.wait_ge(lo_ready, before + (j + 1))
                    s = j % RING
                    for kk in range(2):
                        kt = 2 * j + kk
                        for h in range(HALVES):
                            hs = slice(P * h, P * (h + 1))
                            dst = acc[:, parity, h, :]
                            nc.tensor.matmul(dst, a_hi[:, kt, hs], w_hi[:, s, kk, :],
                                             start=(kt == 0), stop=False)
                            nc.tensor.matmul(dst, a_hi[:, kt, hs], w_lo[:, s, kk, :], start=False, stop=False)
                            last = nc.tensor.matmul(dst, a_lo[:, kt, hs], w_hi[:, s, kk, :],
                                                    start=False, stop=(kt == 2 * pairs - 1))
                    last.then_inc(pair_used, 1)
                    for hook in hooks.get(j, ()):
                        hook()

            def transpose_batch(src, batch):
                if not isinstance(batch, int) or batch > 0:
                    pe.wait_ge(tp_free, batch * 2)
                for b in range(2):
                    for t in range(2):
                        for h in range(HALVES):
                            last = nc.tensor.transpose(tp[:, b, t, P * h:P * (h + 1)], src(2 * b + t, h), ident[:, :])
                    last.then_inc(tp_full, 1)

            def transpose_stage(batch):
                transpose_batch(lambda t, h: stage[:, h, P * t:P * (t + 1)], batch)

            def transpose_block(batch, blk):
                for h in range(HALVES):
                    pe.wait_ge(acc_read[h], blk + 1)
                transpose_stage(batch)

            def transpose_gated(g):
                pe.wait_ge(gated, HALVES * (g + 1))
                transpose_stage(TB_GATED[g])

            def transpose_residual(n):
                for h in range(HALVES):
                    pe.wait_ge(acc_read[h], OUT0 + n + 1)
                transpose_batch(lambda t, h: xres[:, h, NB * n + P * t:NB * n + P * (t + 1)], TB_X2 + n)

            def attn_scores(h):
                pe.wait_ge(tp_free, 2 * (TB_IN[2 + h // 4] + 1))
                if h > 0:
                    pe.wait_ge(sc_free, h)
                nc.tensor.matmul(sc[:, 0:T], qT[:, h, P:T], kT[:, h, :], start=True, stop=True)
                nc.tensor.matmul(sc[:, T:SQ], qT[:, h, 0:P], kT[:, h, 0:P], start=True, stop=True).then_inc(sc_full, 1)

            def attn_transpose(h):
                pe.wait_ge(p_ready, h + 1)
                if h > 0:
                    pe.wait_ge(pT_ready, h)
                pb = probs[:, h % 2, :]
                nc.tensor.transpose(tp_flat[:, 0:P], pb[:, T:SQ], ident[:, :])
                nc.tensor.transpose(tp_flat[:, P:T], pb[:, 0:P], ident[:, :])
                nc.tensor.transpose(tp_flat[:, T:SQ], pb[:, P:T], ident[:, :]).then_inc(pT_full, 1)

            def attn_out(h):
                pe.wait_ge(pT_ready, h + 1)
                for half in range(HALVES):
                    pe.wait_ge(acc_read[half], 4 + h // 4 + 1)
                if h > 0:
                    pe.wait_ge(ot_free, h)
                cols = slice(A_DIM * h, A_DIM * (h + 1))
                nc.tensor.matmul(ot[:, 0:T], va[:, 0, cols], pT[:, h % 2, 0:T], start=True, stop=False)
                nc.tensor.matmul(ot[:, P:T], va[:, 1, cols], pT[:, h % 2, T:SQ], start=False,
                                 stop=True).then_inc(ot_full, 1)

            def ret_scores(h):
                pe.wait_ge(tp_free, 2 * (TB_IN[10 + h // 2] + 1))
                pe.wait_ge(sc_free, A_HEADS + h)
                for dst, i0 in ((sc[:, 0:T], 0), (sc[:, T:SQ], P)):
                    for t in range(2):
                        last = nc.tensor.matmul(dst, kT[:, 2 * h + t, i0:i0 + P], qT[:, 2 * h + t, i0:T],
                                                start=(t == 0), stop=(t == 1))
                last.then_inc(sc_full, 1)

            def ret_out(h):
                pe.wait_ge(sc_free, A_HEADS + h + 1)
                for half in range(HALVES):
                    pe.wait_ge(acc_read[half], 6 + h // 2 + 1)
                pe.wait_ge(ot_free, A_HEADS + h)
                v, a = vr[:, :, R_DIM * h:R_DIM * (h + 1)], probs[:, h % 2, :]
                nc.tensor.matmul(ot[:, 0:R_DIM], a[:, 0:P], v[:, 0, :], start=True, stop=True)
                nc.tensor.matmul(ot[:, R_DIM:], a[:, P:T], v[:, 0, :], start=True, stop=False)
                nc.tensor.matmul(ot[:, R_DIM:], a[:, T:SQ], v[:, 1, :], start=False, stop=True).then_inc(ot_full, 1)

            pe.wait_ge(const_in, 16 * CONSTS)
            nc.tensor.transpose(sc[:, 0:KT], wrow[:, :], ident[0:KT, 0:KT])
            nc.tensor.transpose(sc[:, KT:2 * KT], wrow2[:, :], ident[0:KT, 0:KT]).then_inc(wcol_full, 1)
            for q in range(4):
                pe.wait_ge(x_in[q], 16)
                transpose_batch(lambda t, h: xres[:, h, NB * q + P * t:NB * q + P * (t + 1)], q)

            plan = Plan()
            for b, batch in TB_IN.items():
                if b == 8:
                    plan.put(b + 1, 2, lambda: pe.wait_ge(pT_ready, A_HEADS))
                plan.put(b + 1, 2, lambda b=b, batch=batch: transpose_block(batch, b))
            for h in range(A_HEADS):
                plan.put(0, ATTN_AT + 2 * h, lambda h=h: attn_scores(h))
                plan.put(0, ATTN_AT + 2 * h + 4, lambda h=h: attn_transpose(h))
                plan.put(0, ATTN_AT + 2 * h + 6, lambda h=h: attn_out(h))
            for h in range(R_HEADS):
                plan.put(0, RET_AT[h], lambda h=h: ret_scores(h))
                plan.put(0, RET_AT[h] + 3, lambda h=h: ret_out(h))
            for g in range(2):
                plan.put(13 + g, 3, lambda g=g: transpose_gated(g))
            for n in range(OUT_BLOCKS):
                plan.put(OUT0 + n + 1, 2, lambda n=n: transpose_residual(n))

            def tiles_ready(batch):
                return lambda: pe.wait_ge(tp_free, 2 * (batch + 1))

            def ffn_block(blk, parity, hooks, inputs=None):
                multiply_block(xT_hi, xT_lo, PAIRS, blk * PAIRS, blk, parity, hooks, inputs)

            for b in range(IN_BLOCKS):
                multiply_block(xT_hi, xT_lo, PAIRS, b * PAIRS, b, b % 2, plan.of(b),
                               {2 * q: [tiles_ready(q)] for q in range(4)} if b == 0 else None)
            for b in range(OUT0, FFN0):
                multiply_block(mixT_hi, mixT_lo, PAIRS, b * PAIRS, b, b % 2, plan.of(b),
                               {0: [lambda: pe.wait_ge(ot_free, A_HEADS)],
                                4: [tiles_ready(TB_GATED[0])], 6: [tiles_ready(TB_GATED[1])]} if b == OUT0 else None)
            ffn_block(FFN0, 0, plan.of(FFN0), {2 * q: [tiles_ready(TB_X2 + q)] for q in range(4)})
            ffn_block(FFN0 + 1, 1, {})
            with pe.Fori(1, FFN_STEPS) as i:
                ffn_block(i * 2 + FFN0, 0, {2: [lambda: transpose_block(i + (TB_H - 1), i * 2 + (FFN0 - 1))]})
                ffn_block(i * 2 + (FFN0 + 1), 1, {})
            for n in range(DOWN_BLOCKS):
                multiply_block(hT_hi, hT_lo, DPAIRS, PAIRS * DOWN0 + DPAIRS * n, DOWN0 + n, n % 2,
                               {2: [lambda: transpose_block(TB_H + FFN_STEPS - 1, DOWN0 - 1)]} if n == 0 else {},
                               {0: [tiles_ready(TB_H + FFN_STEPS - 2)],
                                2 * (FFN_STEPS - 1): [tiles_ready(TB_H + FFN_STEPS - 1)]} if n == 0 else None)

        @block.scalar
        def _(act):
            act.dma_start(ident[:, :], ident_c).then_inc(const_in, 16)
            act.dma_start(wrow[:, :], norm_mix_w.rearrange("l (k p) -> (l k) p", p=P)).then_inc(const_in, 16)
            act.dma_start(wrow2[:, :], norm_ffn_w.rearrange("l (k p) -> (l k) p", p=P)).then_inc(const_in, 16)
            act.dma_start(dist[:, :], dist_c).then_inc(const_in, 16)
            act.dma_start(count[:, :], count_c).then_inc(const_in, 16)
            act.dma_start(decay[:, :, :], decay_c).then_inc(const_in, 16)

            def split_block(pairs, before, hooks, landed):
                for j in range(pairs):
                    if j % 2 == 0:
                        landed(j // 2)
                    back = slot_last_user(j, RING, pairs, isinstance(before, int) and before <= PAIRS * DOWN0)
                    if not isinstance(before, int) or before + j >= back:
                        act.wait_ge(pair_used, before + (j - back + 1))
                    nc.scalar.activation(w_hi[:, j % RING, :, :],
                                         raw[:, (j // 2) % RAW, 2 * (j % 2):2 * (j % 2) + 2, :],
                                         ACT.Copy).then_inc(hi_ready, 1)
                    for hook in hooks.get(j, ()):
                        hook()

            def split(blk, hooks):
                split_block(PAIRS, blk * PAIRS, hooks, lambda c: act.wait_ge(raw_in[c], blk * 16 + 16))

            def tiles_hi(dst, kt0, batch, w=None):
                for b in range(2):
                    act.wait_ge(tp_full, batch * 2 + (b + 1))
                    if w is None:
                        nc.scalar.activation(dst[:, bass.ds(kt0 + 2 * b, 2), :], tp[:, b, :, :],
                                             ACT.Copy).then_inc(tp_hi, 1)
                    else:
                        for t in range(2):
                            kt = kt0 + 2 * b + t
                            last = nc.scalar.activation(dst[:, kt, :], tp[:, b, t, :], ACT.Copy,
                                                        scale=w[:, kt:kt + 1])
                        last.then_inc(tp_hi, 1)

            def square(norm, h, q):
                act.wait_ge(sq_done, 8 * norm + 2 * q + h) if norm + q + h > 0 else act.wait_ge(wcol_full, 1)
                if norm == 1 and q + h == 0:
                    act.wait_ge(ret_sq, R_HEADS)
                nc.scalar.activation(junk[:, :], xres[:, h, NB * q:NB * (q + 1)], ACT.Square,
                                     accum_out=sumsq[:, norm, h, q:q + 1]).then_inc(sq_done, 1)

            def block_done(blk):
                act.wait_ge(pair_used, (blk + 1) * PAIRS)

            def read_in_block(b):
                s, n = IN_ORDER[b]
                if b == 0:
                    act.wait_ge(rstd_q_done, 1)
                block_done(b)
                src, cols = acc[:, b % 2, :, :], slice(NB * n, NB * (n + 1))
                if s == GR:
                    for h in range(HALVES):
                        nc.scalar.activation(sgr[:, h, cols], src[:, h, :], ACT.Silu,
                                             scale=rstd[:, 0, h:h + 1]).then_inc(acc_read[h], 1)
                elif s in (VA, VR):
                    dst = va if s == VA else vr
                    nc.scalar.activation(dst[:, 0, cols], src[:, 0, :], ACT.Copy,
                                         scale=rstd[:, 0, 0:1]).then_inc(acc_read[0], 1)
                else:
                    act.wait_ge(tp_full, 2 * TB_IN[b])
                    r = rstd_q[:, 0:1] if s == QA else rstd[:, 0, 0:1]
                    nc.scalar.activation(stage[:, 0, :], src[:, 0, :], ACT.Copy, scale=r).then_inc(acc_read[0], 1)

            def exps(h):
                act.wait_ge(neg_done, h + 1)
                for half, cols in ((1, slice(0, T)), (0, slice(T, SQ))):
                    last = nc.scalar.activation(probs[:, h % 2, cols], probs[:, h % 2, cols], ACT.Exp,
                                                bias=negmax[:, h % 2, half:half + 1])
                last.then_inc(exp_done, 1)

            def copy_pT(h):
                act.wait_ge(pT_full, h + 1)
                if h >= 2:
                    act.wait_ge(ot_full, h - 1)
                nc.scalar.activation(pT[:, h % 2, :], tp_flat[:, 0:SQ], ACT.Copy).then_inc(pT_ready, 1)

            def attn_hi(h):
                act.wait_ge(ot_full, h + 1)
                nc.scalar.activation(mixT_hi[:, h, :], ot[:, 0:T], ACT.Copy).then_inc(ot_hi, 1)

            def ret_squares(h):
                act.wait_ge(ot_full, A_HEADS + h + 1)
                act.wait_ge(ret_sq, h) if h > 0 else act.wait_ge(sq_done, 8)
                for half in range(HALVES):
                    last = nc.scalar.activation(junk[:, R_DIM * half:R_DIM * (half + 1)], ot[:, R_DIM * half:R_DIM * (half + 1)], ACT.Square,
                                                accum_out=rsum[:, h, half:half + 1])
                last.then_inc(ret_sq, 1)

            def residual_squares(norm, q, blk):
                for h in range(HALVES):
                    act.wait_ge(acc_read[h], blk + 1)
                    square(norm, h, q)

            def read_gate(i, blk):
                block_done(blk)
                act.wait_ge(tp_full, (i + TB_H) * 2)
                for h in range(HALVES):
                    nc.scalar.activation(stage[:, h, :], acc[:, 0, h, :], ACT.Silu,
                                         scale=rstd[:, 1, h:h + 1]).then_inc(acc_read[h], 1)

            act.wait_ge(wcol_ready, 2)
            for q in range(4):
                tiles_hi(xT_hi, 4 * q, q, wcol)

            plan = Plan()
            for q in range(4):
                for h in range(HALVES):
                    plan.put(0, 2 * q + h, lambda h=h, q=q: square(0, h, q))
            for b in range(IN_BLOCKS):
                plan.put(b + 1, 3, lambda b=b: read_in_block(b))
            for b, batch in TB_IN.items():
                plan.put(b + 1, 6, lambda b=b, batch=batch: None)
            for h in range(A_HEADS):
                plan.put(0, ATTN_AT + 2 * h + 4, lambda h=h: exps(h))
                plan.put(0, ATTN_AT + 2 * h + 8, lambda h=h: copy_pT(h))
                plan.put(0, ATTN_AT + 2 * h + 10, lambda h=h: attn_hi(h))
            for h in range(R_HEADS):
                plan.put(0, RET_AT[h] + 7, lambda h=h: ret_squares(h))
            for g in range(2):
                plan.put(13 + g, 7, lambda g=g: tiles_hi(mixT_hi, 8 + 4 * g, TB_GATED[g]))
            for n in range(OUT_BLOCKS):
                plan.put(OUT0 + n + 1, 4, lambda n=n: residual_squares(1, n, OUT0 + n))
                plan.put(OUT0 + n + 1, 6, lambda n=n: tiles_hi(xT_hi, 4 * n, TB_X2 + n, wcol2))

            for b in range(FFN0 + 1):
                split(b, plan.of(b))
            act.wait_ge(rstd_done, 2)
            split(FFN0 + 1, {3: [lambda: read_gate(0, FFN0)]})
            with act.Fori(1, FFN_STEPS) as i:
                split(i * 2 + FFN0, {6: [lambda: tiles_hi(hT_hi, (i - 1) * 4, i + (TB_H - 1))]})
                split(i * 2 + (FFN0 + 1), {3: [lambda: read_gate(i, i * 2 + FFN0)]})
            for n in range(DOWN_BLOCKS):
                def landed(c, n=n):
                    uses = slot_uses(c % RAW)
                    act.wait_ge(raw_in[c % RAW], 16 * (DOWN0 + uses * n + c // RAW + 1))
                hooks = {6: [lambda: tiles_hi(hT_hi, (FFN_STEPS - 1) * 4, TB_H + FFN_STEPS - 1)]} if n == 0 else \
                        {3: [lambda n=n: residual_squares(2, n - 1, DOWN0 + n - 1)]}
                split_block(DPAIRS, PAIRS * DOWN0 + DPAIRS * n, hooks, landed)
            residual_squares(2, DOWN_BLOCKS - 1, DOWN0 + DOWN_BLOCKS - 1)
            act.wait_ge(rstd_done, 3)
            act.wait_ge(z_done, 2 * HALVES)
            for h in range(HALVES):
                nc.scalar.activation(xres[:, h, 0:D // 2], xres[:, h, 0:D // 2], ACT.Copy,
                                     scale=rstd[:, 2, h:h + 1]).then_inc(y_act, 1)

        @block.vector
        def _(dve):
            def split_block(pairs, before, hooks):
                for j in range(pairs):
                    dve.wait_ge(hi_ready, before + (j + 1))
                    nc.vector.tensor_tensor(w_lo[:, j % RING, :, :],
                                            raw[:, (j // 2) % RAW, 2 * (j % 2):2 * (j % 2) + 2, :],
                                            w_hi[:, j % RING, :, :].bitcast(F32), ALU.subtract).then_inc(lo_ready, 1)
                    for hook in hooks.get(j, ()):
                        hook()

            def split(blk, hooks):
                split_block(PAIRS, blk * PAIRS, hooks)

            def tiles_lo(dst, src_hi, kt0, batch, w=None):
                for b in range(2):
                    dve.wait_ge(tp_hi, hi_banks(batch) + (b + 1))
                    if w is None:
                        kts = bass.ds(kt0 + 2 * b, 2)
                        nc.vector.tensor_tensor(dst[:, kts, :], tp[:, b, :, :], src_hi[:, kts, :].bitcast(F32),
                                                ALU.subtract).then_inc(tp_free, 1)
                    else:
                        for t in range(2):
                            kt = kt0 + 2 * b + t
                            last = nc.vector.scalar_tensor_tensor(dst[:, kt, :], tp[:, b, t, :], w[:, kt:kt + 1],
                                                                  src_hi[:, kt, :].bitcast(F32),
                                                                  ALU.mult, ALU.subtract)
                        last.then_inc(tp_free, 1)

            def tiles_copy(dst, kt0, batch):
                for b in range(2):
                    dve.wait_ge(tp_full, batch * 2 + (b + 1))
                    nc.vector.tensor_copy(dst[:, kt0 + 2 * b:kt0 + 2 * b + 2, :], tp[:, b, :, :]).then_inc(tp_free, 1)

            def block_done(blk):
                dve.wait_ge(pair_used, (blk + 1) * PAIRS)

            def read_in_block(b):
                s, n = IN_ORDER[b]
                if s == GR:
                    return
                block_done(b)
                src, r = acc[:, b % 2, 1, :], rstd[:, 0, 1:2]
                if s in (VA, VR):
                    dst = (va if s == VA else vr)[:, 1, NB * n:NB * (n + 1)]
                else:
                    dve.wait_ge(tp_full, 2 * TB_IN[b])
                    dst = stage[:, 1, :]
                    if s == QA:
                        r = rstd_q[:, 1:2]
                nc.vector.tensor_scalar(dst, src, r, None, ALU.mult).then_inc(acc_read[1], 1)

            def mean_square(norm, n_squares):
                dve.wait_ge(sq_done, n_squares)
                nc.vector.tensor_reduce(tot[:, norm, :], sumsq[:, norm, :, :], AX_X, ALU.add).then_inc(tot_done, 1)
                dve.wait_ge(tot_done, norm + 1)
                nc.vector.tensor_scalar(meansq[:, norm, :], tot[:, norm, :], 1.0 / D, EPS, ALU.mult,
                                        ALU.add).then_inc(mean_done, 1)

            def query_scale():
                dve.wait_ge(rstd_done, 1)
                nc.vector.tensor_scalar(rstd_q[:, :], rstd[:, 0, :], float(A_DIM) ** -0.5, None,
                                        ALU.mult).then_inc(rstd_q_done, 1)
                dve.wait_ge(rstd_q_done, 1)

            def mask_and_max(h):
                dve.wait_ge(sc_full, h + 1)
                if h >= 2:
                    dve.wait_ge(pT_full, h - 1)
                pb = probs[:, h % 2, :]
                nc.vector.scalar_tensor_tensor(pb, dist[:, :], slopes[h], sc[:, 0:SQ], ALU.mult,
                                               ALU.add).then_inc(sc_free, 1)
                dve.wait_ge(sc_free, h + 1)
                nc.vector.tensor_reduce(rowmax[:, h % 2, 1:2], pb[:, 0:T], AX_X, ALU.max)
                nc.vector.tensor_reduce(rowmax[:, h % 2, 0:1], pb[:, T:SQ], AX_X, ALU.max).then_inc(max_done, 1)
                dve.wait_ge(max_done, h + 1)
                nc.vector.tensor_scalar(negmax[:, h % 2, :], rowmax[:, h % 2, :], -1.0, None,
                                        ALU.mult).then_inc(neg_done, 1)

            def normalise(h):
                dve.wait_ge(exp_done, h + 1)
                halves = ((1, slice(0, T)), (0, slice(T, SQ)))
                pb = probs[:, h % 2, :]
                for half, cols in halves:
                    last = nc.vector.tensor_tensor_reduce(pb[:, cols], pb[:, cols], count[:, cols], 1.0, 0.0,
                                                          ALU.mult, ALU.add, den[:, h % 2, half:half + 1])
                last.then_inc(den_done, 1)
                dve.wait_ge(den_done, h + 1)
                nc.vector.reciprocal(rden[:, h % 2, :], den[:, h % 2, :]).then_inc(rden_done, 1)
                dve.wait_ge(rden_done, h + 1)
                for half, cols in halves:
                    last = nc.vector.tensor_scalar(pb[:, cols], pb[:, cols], rden[:, h % 2, half:half + 1], None,
                                                   ALU.mult)
                last.then_inc(p_ready, 1)

            def attn_lo(h):
                dve.wait_ge(ot_hi, h + 1)
                nc.vector.tensor_tensor(mixT_lo[:, h, :], ot[:, 0:T], mixT_hi[:, h, :].bitcast(F32),
                                        ALU.subtract).then_inc(ot_free, 1)

            def decay_scores(h):
                dve.wait_ge(sc_full, A_HEADS + h + 1)
                if h >= 2:
                    dve.wait_ge(ot_full, A_HEADS + h - 1)
                else:
                    dve.wait_ge(pT_full, A_HEADS)
                nc.vector.tensor_tensor(probs[:, h % 2, :], sc[:, 0:SQ], decay[:, h, :], ALU.mult).then_inc(sc_free, 1)

            def ret_meansq(h):
                dve.wait_ge(ret_sq, h + 1)
                nc.vector.tensor_scalar(rmean[:, h, :], rsum[:, h, :], 1.0 / R_DIM, EPS, ALU.mult,
                                        ALU.add).then_inc(ret_mean, 1)

            def ret_scale(h):
                dve.wait_ge(ret_rstd, h + 1)
                for half in range(HALVES):
                    last = nc.vector.tensor_scalar(retn[:, half, R_DIM * h:R_DIM * (h + 1)],
                                                   ot[:, R_DIM * half:R_DIM * (half + 1)],
                                                   rrstd[:, h, half:half + 1], None, ALU.mult)
                last.then_inc(ot_free, 1)

            def gate(g):
                dve.wait_ge(ot_free, A_HEADS + 2 * (g + 1))
                dve.wait_ge(tp_full, 2 * TB_GATED[g])
                for h in range(HALVES):
                    dve.wait_ge(acc_read[h], 12 + g + 1)
                    cols = slice(NB * g, NB * (g + 1))
                    nc.vector.tensor_tensor(stage[:, h, :], retn[:, h, cols], sgr[:, h, cols],
                                            ALU.mult).then_inc(gated, 1)

            def add_residual(parity, q, blk):
                for h in range(HALVES):
                    cols = xres[:, h, NB * q:NB * (q + 1)]
                    nc.vector.tensor_tensor(cols, acc[:, parity, h, :], cols, ALU.add).then_inc(acc_read[h], 1)

            def read_out_block(n):
                block_done(OUT0 + n)
                if n == 0:
                    dve.wait_ge(sq_done, 8)
                add_residual((OUT0 + n) % 2, n, OUT0 + n)

            def read_up(blk):
                block_done(blk)
                for h in range(HALVES):
                    dve.wait_ge(acc_read[h], blk)
                    nc.vector.scalar_tensor_tensor(stage[:, h, :], acc[:, 1, h, :], rstd[:, 1, h:h + 1],
                                                   stage[:, h, :], ALU.mult, ALU.mult).then_inc(acc_read[h], 1)

            def final_weights(q):
                dve.wait_ge(sq_done, 16 + 2 * (q + 1))
                for h in range(HALVES):
                    cols = slice(NB * q, NB * (q + 1))
                    last = nc.vector.tensor_tensor(xres[:, h, cols], xres[:, h, cols], wfin[:, cols], ALU.mult)
                    last.then_inc(z_done, 1)

            dve.wait_ge(wcol_full, 1)
            nc.vector.tensor_copy(wcol[:, :], sc[:, 0:KT]).then_inc(wcol_ready, 1)
            nc.vector.tensor_copy(wcol2[:, :], sc[:, KT:2 * KT]).then_inc(wcol_ready, 1)
            dve.wait_ge(wcol_ready, 2)
            for q in range(4):
                tiles_lo(xT_lo, xT_hi, 4 * q, q, wcol)

            plan = Plan()
            plan.put(1, 2, lambda: mean_square(0, 8))
            plan.put(1, 3, query_scale)
            for b in range(IN_BLOCKS):
                plan.put(b + 1, 3, lambda b=b: read_in_block(b))
            for b, batch in TB_IN.items():
                s, n = IN_ORDER[b]
                if b == 8:
                    plan.put(b + 1, 6, lambda: dve.wait_ge(sc_full, A_HEADS))
                plan.put(b + 1, 6, lambda s=s, n=n, batch=batch: tiles_copy(qT if s in (QA, QR) else kT, 4 * n, batch))
            for h in range(A_HEADS):
                plan.put(0, ATTN_AT + 2 * h + 4, lambda h=h: mask_and_max(h))
                plan.put(0, ATTN_AT + 2 * h + 5, lambda h=h: normalise(h))
                plan.put(0, ATTN_AT + 2 * h + 10, lambda h=h: attn_lo(h))
            for h in range(R_HEADS):
                plan.put(0, RET_AT[h] + 4, lambda h=h: decay_scores(h))
                plan.put(0, RET_AT[h] + 7, lambda h=h: ret_meansq(h))
                plan.put(0, RET_AT[h] + 8, lambda h=h: ret_scale(h))
            for g in range(2):
                plan.put(13 + g, 4, lambda g=g: gate(g))
                plan.put(13 + g, 7, lambda g=g: tiles_lo(mixT_lo, mixT_hi, 8 + 4 * g, TB_GATED[g]))
            for n in range(OUT_BLOCKS):
                plan.put(OUT0 + n + 1, 3, lambda n=n: read_out_block(n))
                plan.put(OUT0 + n + 1, 6, lambda n=n: tiles_lo(xT_lo, xT_hi, 4 * n, TB_X2 + n, wcol2))
            plan.put(FFN0, 7, lambda: mean_square(1, 16))

            for b in range(FFN0 + 1):
                split(b, plan.of(b))
            dve.wait_ge(rstd_done, 2)
            split(FFN0 + 1, {})
            with dve.Fori(1, FFN_STEPS) as i:
                split(i * 2 + FFN0, {3: [lambda: read_up(i * 2 + (FFN0 - 1))],
                                     6: [lambda: tiles_lo(hT_lo, hT_hi, (i - 1) * 4, i + (TB_H - 1))]})
                split(i * 2 + (FFN0 + 1), {})
            for n in range(DOWN_BLOCKS):
                if n == 0:
                    hooks = {3: [lambda: read_up(DOWN0 - 1)],
                             6: [lambda: tiles_lo(hT_lo, hT_hi, (FFN_STEPS - 1) * 4, TB_H + FFN_STEPS - 1)]}
                else:
                    def read_down(n=n):
                        dve.wait_ge(pair_used, PAIRS * DOWN0 + DPAIRS * n)
                        add_residual((n - 1) % 2, n - 1, DOWN0 + n - 1)

                    def weigh(n=n):
                        if n == 1:
                            dve.wait_ge(wfin_in, 16)
                        final_weights(n - 1)
                    hooks = {2: [read_down], 7: [weigh]}
                split_block(DPAIRS, PAIRS * DOWN0 + DPAIRS * n, hooks)
            q = DOWN_BLOCKS - 1
            dve.wait_ge(pair_used, PAIRS * DOWN0 + DPAIRS * DOWN_BLOCKS)
            add_residual(q % 2, q, DOWN0 + q)
            mean_square(2, 24)
            dve.wait_ge(rstd_done, 3)
            dve.wait_ge(z_done, 3 * HALVES)
            for h in range(HALVES):
                r = rstd[:, 2, h:h + 1]
                c2 = xres[:, h, 2 * NB:3 * NB]
                c3 = xres[:, h, 3 * NB:4 * NB]
                nc.vector.tensor_scalar(c2, c2, r, None, ALU.mult)
                nc.vector.scalar_tensor_tensor(c3, c3, r, wfin[:, 3 * NB:4 * NB], ALU.mult, ALU.mult).then_inc(y_dve, 1)

        @block.gpsimd
        def _(pool):
            nc.gpsimd.memset(mhalf[:, :], -0.5).then_inc(mhalf_ready, 1)
            pool.wait_ge(mhalf_ready, 1)

            def rsqrt(norm):
                pool.wait_ge(mean_done, norm + 1)
                nc.gpsimd.tensor_tensor(rstd[:, norm, :], meansq[:, norm, :], mhalf[:, :], ALU.pow).then_inc(rstd_done, 1)

            rsqrt(0)
            for h in range(R_HEADS):
                pool.wait_ge(ret_mean, h + 1)
                nc.gpsimd.tensor_tensor(rrstd[:, h, :], rmean[:, h, :], mhalf[:, :], ALU.pow).then_inc(ret_rstd, 1)
            rsqrt(1)
            rsqrt(2)


_INS = ["x", "norm_mix_w", "w_in", "w_out", "norm_ffn_w", "w_gate", "w_up", "w_down", "norm_final_w"]


def _tables():
    import numpy as np

    p = np.arange(P)[:, None]
    gap = np.concatenate([P + p - np.arange(T)[None, :], p - np.arange(P)[None, :]], axis=1)
    count = sum(((gap >= 0) & (gap % d == 0) & (gap <= w)).astype(np.float32)
                for w, d in ((128, 1), (512, 4), (2048, 16)))
    dist = np.where(count > 0, -gap, -1e30).astype(np.float32)
    gap = np.concatenate([np.arange(T)[None, :] - p, np.arange(P)[None, :] - p], axis=1).astype(np.float64)
    log_gamma = np.log(1.0 - np.exp2(-5.0 - np.arange(R_HEADS)))
    decay = np.where(gap[:, None, :] >= 0, np.exp(log_gamma[None, :, None] * gap[:, None, :]), 0.0) / R_DIM ** 0.5
    slopes = [2.0 ** (-8.0 * (h + 1) / A_HEADS) for h in range(A_HEADS)]
    return np.eye(P, dtype=np.float32), dist, count.astype(np.float32), decay.astype(np.float32), slopes


def kernel(**inputs):
    import numpy as _np
    import concourse.bacc as _bacc
    from concourse import mybir as _mybir
    from concourse.bass_utils import run_bass_kernel_spmd as _run

    nc = _bacc.Bacc("TRN2", target_bir_lowering=False, num_devices=1)
    *tables, slopes = _tables()
    given = {name: inputs[name] for name in _INS}
    given.update(zip(("ident", "dist", "count", "decay"), tables))
    arrays, args = {}, []
    for name, a in given.items():
        a = _np.ascontiguousarray(a)
        arrays[f"in_{name}_dram"] = a
        args.append(nc.dram_tensor(f"in_{name}_dram", a.shape, _mybir.dt.from_np(a.dtype), kind="ExternalInput").ap())
    args.append(nc.dram_tensor("out_0_dram", (1, T, D), _mybir.dt.float32, kind="ExternalOutput").ap())
    build(nc, *args, slopes)
    r = _run(nc, [arrays], core_ids=[0])
    return r.results[0]["out_0_dram"]
```

```python
import concourse.bass as bass
from concourse import mybir
from contextlib import ExitStack

F32 = mybir.dt.float32
F32R = mybir.dt.float32r
ALU = mybir.AluOpType
ACT = mybir.ActivationFunctionType
AX_X = mybir.AxisListType.X

P = 128
T = 256
HALVES = T // P
D = 2048
NB = 512
KT = D // P
F = 5632
FKT = F // P
A_HEADS, A_DIM = 8, 128
R_HEADS, R_DIM = 4, 256
MIX = 1024
EPS = 1e-6
SQ = 384

WARMING = 2
RAW = 4
RING = 4
AHEAD = 4

IN_BLOCKS, OUT_BLOCKS, FFN_STEPS, DOWN_BLOCKS = 14, D // NB, F // NB, D // NB
PAIRS = KT // 2
DPAIRS = FKT // 2
CHUNKS, DCHUNKS = PAIRS // 2, DPAIRS // 2
OUT0 = IN_BLOCKS
FFN0 = OUT0 + OUT_BLOCKS
DOWN0 = FFN0 + 2 * FFN_STEPS

QA, KA, VA, QR, KR, VR, GR = range(7)
IN_ORDER = [(s, n) for s in (QA, KA, VA, VR, KR, QR, GR) for n in range(2)]


ATTN_AT = 41
RET_AT = (96, 98, 104, 106)

TB_IN = {b: 4 + i for i, b in enumerate(b for b, (s, _) in enumerate(IN_ORDER) if s in (QA, KA, KR, QR))}
TB_GATED = [4 + len(TB_IN), 5 + len(TB_IN)]
TB_X2 = TB_GATED[1] + 1
TB_H = TB_X2 + 4


def hi_banks(batch):
    return batch * 2 if isinstance(batch, int) and batch < 4 else batch * 2 - 2 * len(TB_IN)


def slot_uses(slot):
    return len(range(slot, DCHUNKS, RAW))


class Plan:

    def __init__(self):
        self.after = {}

    def put(self, blk, pair, work):
        self.after.setdefault(PAIRS * blk + pair, []).append(work)

    def of(self, blk):
        return {j: self.after[PAIRS * blk + j] for j in range(PAIRS) if PAIRS * blk + j in self.after}


def slot_last_user(j, slots, per_block, first_block):
    if j >= slots or first_block or per_block % slots == 0:
        return slots
    last = max(k for k in range(per_block) if k % slots == j)
    return per_block + j - last


def build(nc, x, norm_mix_w, w_in, w_out, norm_ffn_w, w_gate, w_up, w_down, norm_final_w,
          ident_c, dist_c, count_c, decay_c, out, slopes):
    base = -(-nc.sbuf_base // 64) * 64

    def place(name, shape, dt, offset):
        return nc.alloc_sbuf_tensor_at(name, shape, dt, offset=base + offset)

    KB = 1024
    xT_hi = place("xT_hi", [P, KT, T], F32R, 0)
    xT_lo = place("xT_lo", [P, KT, T], F32R, 16 * KB)
    wfin = place("wfin", [P, D], F32, 0)
    xres = place("xres", [P, HALVES, D], F32, 32 * KB)
    region = 48 * KB
    hT_hi = place("hT_hi", [P, FKT, T], F32R, region)
    hT_lo = place("hT_lo", [P, FKT, T], F32R, region + 44 * KB)
    mixT_hi = place("mixT_hi", [P, KT, T], F32R, region)
    mixT_lo = place("mixT_lo", [P, KT, T], F32R, region + 16 * KB)
    qT = place("qT", [P, MIX // P, T], F32, region + 32 * KB)
    kT = place("kT", [P, MIX // P, T], F32, region + 40 * KB)
    va = place("va", [P, HALVES, MIX], F32, region + 48 * KB)
    retn = place("retn", [P, HALVES, MIX], F32, region + 48 * KB)
    vr = place("vr", [P, HALVES, MIX], F32, region + 56 * KB)
    sgr = place("sgr", [P, HALVES, MIX], F32, region + 64 * KB)
    dist = place("dist", [P, SQ], F32, region + 72 * KB)
    count = place("count", [P, SQ], F32, region + 72 * KB + 1536)
    decay = place("decay", [P, R_HEADS, SQ], F32, region + 75 * KB)
    probs = place("probs", [P, 2, SQ], F32, region + 81 * KB)
    pT = place("pT", [P, 2, SQ], F32, region + 84 * KB)
    raw = place("raw", [P, RAW, 4, NB], F32, 136 * KB)
    w_hi = place("w_hi", [P, RING, 2, NB], F32R, 168 * KB)
    w_lo = place("w_lo", [P, RING, 2, NB], F32R, 184 * KB)
    stage = place("stage", [P, HALVES, NB], F32, 200 * KB)
    small_at = [204 * KB]

    def small(name, shape, dt=F32):
        n = 4
        for d in shape[1:]:
            n *= d
        offset = small_at[0]
        small_at[0] += -(-n // 32) * 32
        return place(name, shape, dt, offset)

    wrow = place("wrow", [KT, P], F32, 200 * KB)
    wrow2 = place("wrow2", [KT, P], F32, 200 * KB + 512)
    junk = small("junk", [P, NB])
    ident = small("ident", [P, P])
    wcol = small("wcol", [P, KT])
    wcol2 = small("wcol2", [P, KT])
    sumsq = small("sumsq", [P, 3, HALVES, 4])
    tot = small("tot", [P, 3, HALVES])
    meansq = small("meansq", [P, 3, HALVES])
    rstd = small("rstd", [P, 3, HALVES])
    rstd_q = small("rstd_q", [P, HALVES])
    mhalf = small("mhalf", [P, HALVES])
    rowmax = small("rowmax", [P, 2, HALVES])
    negmax = small("negmax", [P, 2, HALVES])
    den = small("den", [P, 2, HALVES])
    rden = small("rden", [P, 2, HALVES])
    rsum = small("rsum", [P, R_HEADS, HALVES])
    rmean = small("rmean", [P, R_HEADS, HALVES])
    rrstd = small("rrstd", [P, R_HEADS, HALVES])

    x_d = x.rearrange("b (h p) d -> (b p) h d", p=P)
    out_d = out.rearrange("b (h p) d -> (b p) h d", p=P)
    w_in_d = w_in.rearrange("l (k p) n -> (l p) k n", p=P)
    w_out_d = w_out.rearrange("l (k p) n -> (l p) k n", p=P)
    w_gate_d = w_gate.rearrange("l (k p) n -> (l p) k n", p=P)
    w_up_d = w_up.rearrange("l (k p) n -> (l p) k n", p=P)
    w_down_d = w_down.rearrange("l (k p) n -> (l p) k n", p=P)

    with ExitStack() as ctx:
        def sem(name):
            return ctx.enter_context(nc.semaphore(name))

        def bank(name, shape):
            return ctx.enter_context(nc.psum_tensor(name, shape, F32))

        acc = bank("acc", [P, 2, HALVES, NB])
        tp = bank("tp", [P, 2, 2, T])
        sc = bank("sc", [P, NB])
        ot = bank("ot", [P, NB])

        norm_in = sem("norm_in")
        const_in = sem("const_in")
        x_in = [sem(f"x_in{j}") for j in range(PAIRS)]
        wfin_in = sem("wfin_in")
        early_in = [sem(f"early_in{c}") for c in range(CHUNKS)]
        raw_in = [sem(f"raw_in{s}") for s in range(RAW)]
        hi_ready = sem("hi_ready")
        lo_ready = sem("lo_ready")
        pair_used = sem("pair_used")
        acc_read = [sem(f"acc_read{h}") for h in range(HALVES)]
        tp_full = sem("tp_full")
        tp_hi = sem("tp_hi")
        tp_free = sem("tp_free")
        junk_ready = sem("junk_ready")
        table_ready = sem("table_ready")
        warm = sem("warm")
        wcol_full = sem("wcol_full")
        wcol_ready = sem("wcol_ready")
        mhalf_ready = sem("mhalf_ready")
        sq_done = sem("sq_done")
        tot_done = sem("tot_done")
        mean_done = sem("mean_done")
        rstd_done = sem("rstd_done")
        rstd_q_done = sem("rstd_q_done")
        sc_full = sem("sc_full")
        sc_free = sem("sc_free")
        max_done = sem("max_done")
        neg_done = sem("neg_done")
        exp_done = sem("exp_done")
        den_done = sem("den_done")
        rden_done = sem("rden_done")
        p_ready = sem("p_ready")
        pT_full = sem("pT_full")
        pT_ready = sem("pT_ready")
        ot_full = sem("ot_full")
        ot_hi = sem("ot_hi")
        ot_free = sem("ot_free")
        ret_sq = sem("ret_sq")
        ret_mean = sem("ret_mean")
        ret_rstd = sem("ret_rstd")
        gated = sem("gated")
        z_done = sem("z_done")
        last_full = sem("last_full")
        y_act = sem("y_act")
        y_dve = sem("y_dve")
        out_done = sem("out_done")

        tp_flat = tp[:, 0, :, :].rearrange("p a b -> p (a b)")
        block = ctx.enter_context(nc.Block())

        @block.sync
        def _(sp):
            sp.dma_start(ident[:, :], ident_c).then_inc(norm_in, 16)
            for j in range(PAIRS):
                cols = slice(2 * P * j, 2 * P * (j + 1))
                sp.dma_start(xres[:, :, cols], x_d[:, :, cols]).then_inc(x_in[j], 16)
                sp.dma_start(raw[:, j // 2, 2 * (j % 2):2 * (j % 2) + 2, :], w_in_d[:, 2 * j:2 * j + 2, 0:NB]
                             ).then_inc(raw_in[j // 2] if j % 2 else early_in[j // 2], 16)

            def load_block(w, col, blk):
                for c in range(CHUNKS):
                    sp.wait_ge(lo_ready, blk * PAIRS + (2 * c + 2 - PAIRS))
                    sp.dma_start(raw[:, c, :, :], w[:, 4 * c:4 * c + 4, bass.ds(col, NB)]).then_inc(raw_in[c], 16)

            for b, (s, n) in list(enumerate(IN_ORDER))[1:]:
                load_block(w_in_d, MIX * s + NB * n, b)
            for n in range(OUT_BLOCKS):
                load_block(w_out_d, NB * n, OUT0 + n)
            with sp.Fori(0, FFN_STEPS) as i:
                load_block(w_gate_d, i * NB, i * 2 + FFN0)
                load_block(w_up_d, i * NB, i * 2 + (FFN0 + 1))

            def load_down(n):
                for c in range(DCHUNKS):
                    back = slot_last_user(c, RAW, DCHUNKS, isinstance(n, int) and n == 0)
                    sp.wait_ge(lo_ready, n * DPAIRS + (PAIRS * DOWN0 + 2 * (c - back) + 2))
                    sp.dma_start(raw[:, c % RAW, :, :],
                                 w_down_d[:, 4 * c:4 * c + 4, bass.ds(n * NB, NB)]).then_inc(raw_in[c % RAW], 16)

            load_down(0)
            sp.wait_ge(pair_used, PAIRS * DOWN0)
            sp.dma_start(wfin[:, :], norm_final_w.partition_broadcast(P)).then_inc(wfin_in, 16)
            with sp.Fori(1, DOWN_BLOCKS) as n:
                load_down(n)
            for h in range(HALVES):
                for k in range(2):
                    for q, done in ((2 + k, y_dve), (k, y_act)):
                        sp.wait_ge(done, 2 * h + k + 1)
                        cols = slice(NB * q, NB * (q + 1))
                        sp.dma_start(out_d[:, h, cols], xres[:, h, cols]).then_inc(out_done, 16)
            sp.wait_ge(out_done, 16 * 4 * HALVES)

        @block.tensor
        def _(pe):
            def multiply_pair(a_hi, a_lo, pairs, parity, j, halves):
                for kk in range(2):
                    kt = 2 * j + kk
                    for h in halves:
                        hs = slice(P * h, P * (h + 1))
                        dst = acc[:, parity, h, :]
                        hi, lo = w_hi[:, j % RING, kk, :], w_lo[:, j % RING, kk, :]
                        nc.tensor.matmul(dst, a_hi[:, kt, hs], hi, start=(kt == 0), stop=False)
                        nc.tensor.matmul(dst, a_hi[:, kt, hs], lo, start=False, stop=False)
                        last = nc.tensor.matmul(dst, a_lo[:, kt, hs], hi, start=False, stop=(kt == 2 * pairs - 1))
                return last

            def multiply_block(a_hi, a_lo, pairs, before, blk, parity, hooks, inputs=None, last=False):
                if not isinstance(blk, int) or blk >= 2:
                    for h in range(HALVES):
                        pe.wait_ge(acc_read[h], blk - 1)
                for j in range(pairs - RING if last else pairs):
                    for wait in (inputs or {}).get(j, ()):
                        wait()
                    pe.wait_ge(lo_ready, before + (j + 1))
                    multiply_pair(a_hi, a_lo, pairs, parity, j, range(HALVES)).then_inc(pair_used, 1)
                    for hook in hooks.get(j, ()):
                        hook()

                if last:
                    for h in range(HALVES):
                        for j in range(pairs - RING, pairs):
                            pe.wait_ge(lo_ready, before + (j + 1))
                            mm = multiply_pair(a_hi, a_lo, pairs, parity, j, (h,))
                        mm.then_inc(last_full, 1)

            def transpose_batch(src, batch, banks=range(2)):
                for b in banks:
                    if not isinstance(batch, int) or batch > 0:
                        pe.wait_ge(tp_free, batch * 2 + (b - 1))
                    for t in range(2):
                        for h in range(HALVES):
                            last = nc.tensor.transpose(tp[:, b, t, P * h:P * (h + 1)], src(2 * b + t, h), ident[:, :])
                    last.then_inc(tp_full, 1)

            def transpose_stage(batch):
                transpose_batch(lambda t, h: stage[:, h, P * t:P * (t + 1)], batch)

            def transpose_block(batch, blk):
                for h in range(HALVES):
                    pe.wait_ge(acc_read[h], blk + 1)
                transpose_stage(batch)

            def transpose_gated(g):
                pe.wait_ge(gated, HALVES * (g + 1))
                transpose_stage(TB_GATED[g])

            def transpose_residual(n):
                for h in range(HALVES):
                    pe.wait_ge(acc_read[h], OUT0 + n + 1)
                transpose_batch(lambda t, h: xres[:, h, NB * n + P * t:NB * n + P * (t + 1)], TB_X2 + n)

            def attn_scores(h):
                pe.wait_ge(tp_free, 2 * (TB_IN[2 + h // 4] + 1))
                if h > 0:
                    pe.wait_ge(sc_free, h)
                nc.tensor.matmul(sc[:, 0:T], qT[:, h, P:T], kT[:, h, :], start=True, stop=True)
                nc.tensor.matmul(sc[:, T:SQ], qT[:, h, 0:P], kT[:, h, 0:P], start=True, stop=True).then_inc(sc_full, 1)

            def attn_transpose(h):
                pe.wait_ge(p_ready, h + 1)
                if h > 0:
                    pe.wait_ge(pT_ready, h)
                pb = probs[:, h % 2, :]
                nc.tensor.transpose(tp_flat[:, 0:P], pb[:, T:SQ], ident[:, :])
                nc.tensor.transpose(tp_flat[:, P:T], pb[:, 0:P], ident[:, :])
                nc.tensor.transpose(tp_flat[:, T:SQ], pb[:, P:T], ident[:, :]).then_inc(pT_full, 1)

            def attn_out(h):
                pe.wait_ge(pT_ready, h + 1)
                for half in range(HALVES):
                    pe.wait_ge(acc_read[half], 4 + h // 4 + 1)
                if h > 0:
                    pe.wait_ge(ot_free, h)
                cols = slice(A_DIM * h, A_DIM * (h + 1))
                nc.tensor.matmul(ot[:, 0:T], va[:, 0, cols], pT[:, h % 2, 0:T], start=True, stop=False)
                nc.tensor.matmul(ot[:, P:T], va[:, 1, cols], pT[:, h % 2, T:SQ], start=False,
                                 stop=True).then_inc(ot_full, 1)

            def ret_scores(h):
                pe.wait_ge(tp_free, 2 * (TB_IN[10 + h // 2] + 1))
                pe.wait_ge(sc_free, A_HEADS + h)
                for dst, i0 in ((sc[:, 0:T], 0), (sc[:, T:SQ], P)):
                    for t in range(2):
                        last = nc.tensor.matmul(dst, kT[:, 2 * h + t, i0:i0 + P], qT[:, 2 * h + t, i0:T],
                                                start=(t == 0), stop=(t == 1))
                last.then_inc(sc_full, 1)

            def ret_out(h):
                pe.wait_ge(sc_free, A_HEADS + h + 1)
                for half in range(HALVES):
                    pe.wait_ge(acc_read[half], 6 + h // 2 + 1)
                pe.wait_ge(ot_free, A_HEADS + h)
                v, a = vr[:, :, R_DIM * h:R_DIM * (h + 1)], probs[:, h % 2, :]
                nc.tensor.matmul(ot[:, 0:R_DIM], a[:, 0:P], v[:, 0, :], start=True, stop=True)
                nc.tensor.matmul(ot[:, R_DIM:], a[:, P:T], v[:, 0, :], start=True, stop=False)
                nc.tensor.matmul(ot[:, R_DIM:], a[:, T:SQ], v[:, 1, :], start=False, stop=True).then_inc(ot_full, 1)

            pe.wait_ge(junk_ready, 1)
            for _ in range(WARMING):
                mm = nc.tensor.matmul(ot[:, :], junk[:, 0:P], junk[:, :], start=True, stop=True)
            mm.then_inc(warm, 1)
            pe.wait_ge(norm_in, 16 * 3)
            nc.tensor.transpose(sc[:, 0:KT], wrow[:, :], ident[0:KT, 0:KT])
            nc.tensor.transpose(sc[:, KT:2 * KT], wrow2[:, :], ident[0:KT, 0:KT]).then_inc(wcol_full, 1)

            def transpose_input(j):
                pe.wait_ge(x_in[j], 16)
                transpose_batch(lambda t, h: xres[:, h, NB * (j // 2) + P * t:NB * (j // 2) + P * (t + 1)],
                                j // 2, (j % 2,))

            for j in range(3):
                transpose_input(j)

            plan = Plan()
            for j in range(3, PAIRS):
                plan.put(0, j - 3, lambda j=j: transpose_input(j))
            for b, batch in TB_IN.items():
                if b == 8:
                    plan.put(b + 1, 2, lambda: pe.wait_ge(pT_ready, A_HEADS))
                plan.put(b + 1, 2, lambda b=b, batch=batch: transpose_block(batch, b))
            for h in range(A_HEADS):
                plan.put(0, ATTN_AT + 3 * h, lambda h=h: attn_scores(h))
                plan.put(0, ATTN_AT + 3 * h + 4, lambda h=h: attn_transpose(h))
                plan.put(0, ATTN_AT + 3 * h + 6, lambda h=h: attn_out(h))
            for h in range(R_HEADS):
                plan.put(0, RET_AT[h], lambda h=h: ret_scores(h))
                plan.put(0, RET_AT[h] + 3, lambda h=h: ret_out(h))
            for g in range(2):
                plan.put(13 + g, 3, lambda g=g: transpose_gated(g))
            for n in range(OUT_BLOCKS):
                plan.put(OUT0 + n + 1, 2, lambda n=n: transpose_residual(n))

            def tiles_ready(batch):
                return lambda: pe.wait_ge(tp_free, 2 * (batch + 1))

            def ffn_block(blk, parity, hooks, inputs=None):
                multiply_block(xT_hi, xT_lo, PAIRS, blk * PAIRS, blk, parity, hooks, inputs)

            for b in range(IN_BLOCKS):
                multiply_block(xT_hi, xT_lo, PAIRS, b * PAIRS, b, b % 2, plan.of(b),
                               {j: [lambda j=j: pe.wait_ge(tp_free, j + 1)] for j in range(PAIRS)} if b == 0 else None)
            for b in range(OUT0, FFN0):
                multiply_block(mixT_hi, mixT_lo, PAIRS, b * PAIRS, b, b % 2, plan.of(b),
                               {0: [lambda: pe.wait_ge(ot_free, A_HEADS)],
                                4: [tiles_ready(TB_GATED[0])], 6: [tiles_ready(TB_GATED[1])]} if b == OUT0 else None)
            ffn_block(FFN0, 0, plan.of(FFN0), {2 * q: [tiles_ready(TB_X2 + q)] for q in range(4)})
            ffn_block(FFN0 + 1, 1, {})
            with pe.Fori(1, FFN_STEPS) as i:
                ffn_block(i * 2 + FFN0, 0, {2: [lambda: transpose_block(i + (TB_H - 1), i * 2 + (FFN0 - 1))]})
                ffn_block(i * 2 + (FFN0 + 1), 1, {})
            def down_block(n, parity, hooks, inputs=None, last=False):
                multiply_block(hT_hi, hT_lo, DPAIRS, n * DPAIRS + PAIRS * DOWN0, n + DOWN0, parity, hooks, inputs, last)

            down_block(0, 0, {2: [lambda: transpose_block(TB_H + FFN_STEPS - 1, DOWN0 - 1)]},
                       {0: [tiles_ready(TB_H + FFN_STEPS - 2)],
                        2 * (FFN_STEPS - 1): [tiles_ready(TB_H + FFN_STEPS - 1)]})
            with pe.Fori(1, DOWN_BLOCKS - 1) as n:
                down_block(n, n * -1 + 2, {})
            down_block(DOWN_BLOCKS - 1, 1, {}, last=True)

        @block.scalar
        def _(act):
            act.dma_start(wrow[:, :], norm_mix_w.rearrange("l (k p) -> (l k) p", p=P)).then_inc(norm_in, 16)
            act.dma_start(wrow2[:, :], norm_ffn_w.rearrange("l (k p) -> (l k) p", p=P)).then_inc(norm_in, 16)

            act.wait_ge(junk_ready, 1)
            nc.scalar.activation(sumsq[:, 0, 0, 0:1], junk[:, 0:1], ACT.Copy).then_inc(table_ready, 1)

            def load_tables():
                act.dma_start(dist[:, :], dist_c).then_inc(const_in, 16)
                act.dma_start(count[:, :], count_c).then_inc(const_in, 16)
                act.dma_start(decay[:, :, :], decay_c).then_inc(const_in, 16)

            def split_block(pairs, before, hooks, landed, ahead=None):
                for j in range(pairs):
                    for work in (ahead or {}).get(j, ()):
                        work()
                    landed(j)
                    back = slot_last_user(j, RING, pairs, isinstance(before, int) and before <= PAIRS * DOWN0)
                    if not isinstance(before, int) or before + j >= back:
                        act.wait_ge(pair_used, before + (j - back + 1))
                    nc.scalar.activation(w_hi[:, j % RING, :, :],
                                         raw[:, (j // 2) % RAW, 2 * (j % 2):2 * (j % 2) + 2, :],
                                         ACT.Copy).then_inc(hi_ready, 1)
                    for hook in hooks.get(j, ()):
                        hook()

            def split(blk, hooks, ahead=None):
                def landed(j):
                    if j % 2 == 0:
                        act.wait_ge(raw_in[j // 2], blk * 16 + 16)

                def landed_early(j):
                    act.wait_ge(raw_in[j // 2] if j % 2 else early_in[j // 2], 16)

                first = isinstance(blk, int) and blk == 0
                split_block(PAIRS, blk * PAIRS, hooks, landed_early if first else landed, ahead)

            def tiles_hi(dst, kt0, batch, w=None, banks=range(2)):
                for b in banks:
                    act.wait_ge(tp_full, batch * 2 + (b + 1))
                    if w is None:
                        nc.scalar.activation(dst[:, bass.ds(kt0 + 2 * b, 2), :], tp[:, b, :, :],
                                             ACT.Copy).then_inc(tp_hi, 1)
                    else:
                        for t in range(2):
                            kt = kt0 + 2 * b + t
                            last = nc.scalar.activation(dst[:, kt, :], tp[:, b, t, :], ACT.Copy,
                                                        scale=w[:, kt:kt + 1])
                        last.then_inc(tp_hi, 1)

            def square(norm, h, q):
                if isinstance(q, int) and norm + q + h == 0:
                    act.wait_ge(warm, 1)
                    act.wait_ge(table_ready, 1)
                else:
                    act.wait_ge(sq_done, q * 2 + (8 * norm + h))
                if norm == 1 and q + h == 0:
                    act.wait_ge(ret_sq, R_HEADS)
                nc.scalar.activation(junk[:, :], xres[:, h, bass.ds(q * NB, NB)], ACT.Square,
                                     accum_out=sumsq[:, norm, h, bass.ds(q, 1)]).then_inc(sq_done, 1)

            def block_done(blk):
                act.wait_ge(pair_used, (blk + 1) * PAIRS)

            def read_in_block(b):
                s, n = IN_ORDER[b]
                if b == 0:
                    act.wait_ge(rstd_q_done, 1)
                block_done(b)
                src, cols = acc[:, b % 2, :, :], slice(NB * n, NB * (n + 1))
                if s == GR:
                    for h in range(HALVES):
                        nc.scalar.activation(sgr[:, h, cols], src[:, h, :], ACT.Silu,
                                             scale=rstd[:, 0, h:h + 1]).then_inc(acc_read[h], 1)
                elif s in (VA, VR):
                    dst = va if s == VA else vr
                    nc.scalar.activation(dst[:, 0, cols], src[:, 0, :], ACT.Copy,
                                         scale=rstd[:, 0, 0:1]).then_inc(acc_read[0], 1)
                else:
                    act.wait_ge(tp_full, 2 * TB_IN[b])
                    r = rstd_q[:, 0:1] if s == QA else rstd[:, 0, 0:1]
                    nc.scalar.activation(stage[:, 0, :], src[:, 0, :], ACT.Copy, scale=r).then_inc(acc_read[0], 1)

            def exps(h):
                act.wait_ge(neg_done, h + 1)
                for half, cols in ((1, slice(0, T)), (0, slice(T, SQ))):
                    last = nc.scalar.activation(probs[:, h % 2, cols], probs[:, h % 2, cols], ACT.Exp,
                                                bias=negmax[:, h % 2, half:half + 1])
                last.then_inc(exp_done, 1)

            def copy_pT(h):
                act.wait_ge(pT_full, h + 1)
                if h >= 2:
                    act.wait_ge(ot_full, h - 1)
                nc.scalar.activation(pT[:, h % 2, :], tp_flat[:, 0:SQ], ACT.Copy).then_inc(pT_ready, 1)

            def attn_hi(h):
                act.wait_ge(ot_full, h + 1)
                nc.scalar.activation(mixT_hi[:, h, :], ot[:, 0:T], ACT.Copy).then_inc(ot_hi, 1)

            def ret_squares(h):
                act.wait_ge(ot_full, A_HEADS + h + 1)
                act.wait_ge(ret_sq, h) if h > 0 else act.wait_ge(sq_done, 8)
                for half in range(HALVES):
                    last = nc.scalar.activation(junk[:, R_DIM * half:R_DIM * (half + 1)], ot[:, R_DIM * half:R_DIM * (half + 1)], ACT.Square,
                                                accum_out=rsum[:, h, half:half + 1])
                last.then_inc(ret_sq, 1)

            def residual_squares(norm, q, blk):
                for h in range(HALVES):
                    act.wait_ge(acc_read[h], blk + 1)
                    square(norm, h, q)

            def read_gate(i, blk):
                block_done(blk)
                act.wait_ge(tp_full, (i + TB_H) * 2)
                for h in range(HALVES):
                    nc.scalar.activation(stage[:, h, :], acc[:, 0, h, :], ACT.Silu,
                                         scale=rstd[:, 1, h:h + 1]).then_inc(acc_read[h], 1)

            act.wait_ge(wcol_ready, 2)
            plan = Plan()
            plan.put(0, 5, load_tables)
            for q in range(4):
                for h in range(HALVES):
                    plan.put(0, 6 + q, lambda h=h, q=q: square(0, h, q))
            for b in range(IN_BLOCKS):
                plan.put(b + 1, 3, lambda b=b: read_in_block(b))
            for h in range(A_HEADS):
                plan.put(0, ATTN_AT + 3 * h + 4, lambda h=h: exps(h))
                plan.put(0, ATTN_AT + 3 * h + 8, lambda h=h: copy_pT(h))
                plan.put(0, ATTN_AT + 3 * h + 10, lambda h=h: attn_hi(h))
            for h in range(R_HEADS):
                plan.put(0, RET_AT[h] + 7, lambda h=h: ret_squares(h))
            for g in range(2):
                plan.put(13 + g, 7, lambda g=g: tiles_hi(mixT_hi, 8 + 4 * g, TB_GATED[g]))
            for n in range(OUT_BLOCKS):
                plan.put(OUT0 + n + 1, 4, lambda n=n: residual_squares(1, n, OUT0 + n))
                plan.put(OUT0 + n + 1, 6, lambda n=n: tiles_hi(xT_hi, 4 * n, TB_X2 + n, wcol2))

            for b in range(FFN0 + 1):
                split(b, plan.of(b), {j: [lambda j=j: tiles_hi(xT_hi, 4 * (j // 2), j // 2, wcol, (j % 2,))]
                                      for j in range(PAIRS)} if b == 0 else None)
            act.wait_ge(rstd_done, 2)
            split(FFN0 + 1, {3: [lambda: read_gate(0, FFN0)]})
            with act.Fori(1, FFN_STEPS) as i:
                split(i * 2 + FFN0, {6: [lambda: tiles_hi(hT_hi, (i - 1) * 4, i + (TB_H - 1))]})
                split(i * 2 + (FFN0 + 1), {3: [lambda: read_gate(i, i * 2 + FFN0)]})

            def split_down(n, hooks):
                def landed(j):
                    slot, use = j // 2 % RAW, j // 2 // RAW
                    if j % 2 == 0:
                        act.wait_ge(raw_in[slot], n * (16 * slot_uses(slot)) + 16 * (DOWN0 + use + 1))

                split_block(DPAIRS, n * DPAIRS + PAIRS * DOWN0, hooks, landed)

            split_down(0, {6: [lambda: tiles_hi(hT_hi, (FFN_STEPS - 1) * 4, TB_H + FFN_STEPS - 1)]})
            with act.Fori(1, DOWN_BLOCKS) as n:
                split_down(n, {3: [lambda: residual_squares(2, n - 1, n + (DOWN0 - 1))]})
            for h in range(HALVES):
                act.wait_ge(acc_read[h], DOWN0 + DOWN_BLOCKS)
                square(2, h, DOWN_BLOCKS - 1)
                act.wait_ge(rstd_done, 3 + h)
                act.wait_ge(z_done, 2 * HALVES)
                for q in range(2):
                    cols = xres[:, h, NB * q:NB * (q + 1)]
                    nc.scalar.activation(cols, cols, ACT.Copy, scale=rstd[:, 2, h:h + 1]).then_inc(y_act, 1)

        @block.vector
        def _(dve):
            def split_block(pairs, before, hooks, ahead=None):
                for j in range(pairs):
                    for work in (ahead or {}).get(j, ()):
                        work()
                    dve.wait_ge(hi_ready, before + (j + 1))
                    nc.vector.tensor_tensor(w_lo[:, j % RING, :, :],
                                            raw[:, (j // 2) % RAW, 2 * (j % 2):2 * (j % 2) + 2, :],
                                            w_hi[:, j % RING, :, :].bitcast(F32), ALU.subtract).then_inc(lo_ready, 1)
                    for hook in hooks.get(j, ()):
                        hook()

            def split(blk, hooks, ahead=None):
                split_block(PAIRS, blk * PAIRS, hooks, ahead)

            def tiles_lo(dst, src_hi, kt0, batch, w=None, banks=range(2)):
                for b in banks:
                    dve.wait_ge(tp_hi, hi_banks(batch) + (b + 1))
                    if w is None:
                        kts = bass.ds(kt0 + 2 * b, 2)
                        nc.vector.tensor_tensor(dst[:, kts, :], tp[:, b, :, :], src_hi[:, kts, :].bitcast(F32),
                                                ALU.subtract).then_inc(tp_free, 1)
                    else:
                        for t in range(2):
                            kt = kt0 + 2 * b + t
                            last = nc.vector.scalar_tensor_tensor(dst[:, kt, :], tp[:, b, t, :], w[:, kt:kt + 1],
                                                                  src_hi[:, kt, :].bitcast(F32),
                                                                  ALU.mult, ALU.subtract)
                        last.then_inc(tp_free, 1)

            def tiles_copy(dst, kt0, batch):
                for b in range(2):
                    dve.wait_ge(tp_full, batch * 2 + (b + 1))
                    nc.vector.tensor_copy(dst[:, kt0 + 2 * b:kt0 + 2 * b + 2, :], tp[:, b, :, :]).then_inc(tp_free, 1)

            def block_done(blk):
                dve.wait_ge(pair_used, (blk + 1) * PAIRS)

            def read_in_block(b):
                s, n = IN_ORDER[b]
                if s == GR:
                    return
                block_done(b)
                src, r = acc[:, b % 2, 1, :], rstd[:, 0, 1:2]
                if s in (VA, VR):
                    dst = (va if s == VA else vr)[:, 1, NB * n:NB * (n + 1)]
                else:
                    dve.wait_ge(tp_full, 2 * TB_IN[b])
                    dst = stage[:, 1, :]
                    if s == QA:
                        r = rstd_q[:, 1:2]
                nc.vector.tensor_scalar(dst, src, r, None, ALU.mult).then_inc(acc_read[1], 1)

            def mean_square(norm, n_squares, hs=slice(0, HALVES), n=None):
                n = norm if n is None else n
                dve.wait_ge(sq_done, n_squares)
                nc.vector.tensor_reduce(tot[:, norm, hs], sumsq[:, norm, hs, :], AX_X, ALU.add).then_inc(tot_done, 1)
                dve.wait_ge(tot_done, n + 1)
                nc.vector.tensor_scalar(meansq[:, norm, hs], tot[:, norm, hs], 1.0 / D, EPS, ALU.mult,
                                        ALU.add).then_inc(mean_done, 1)

            def query_scale():
                dve.wait_ge(rstd_done, 1)
                nc.vector.tensor_scalar(rstd_q[:, :], rstd[:, 0, :], float(A_DIM) ** -0.5, None,
                                        ALU.mult).then_inc(rstd_q_done, 1)
                dve.wait_ge(rstd_q_done, 1)

            def mask_and_max(h):
                if h == 0:
                    dve.wait_ge(const_in, 16 * 3)
                dve.wait_ge(sc_full, h + 1)
                if h >= 2:
                    dve.wait_ge(pT_full, h - 1)
                pb = probs[:, h % 2, :]
                nc.vector.scalar_tensor_tensor(pb, dist[:, :], slopes[h], sc[:, 0:SQ], ALU.mult,
                                               ALU.add).then_inc(sc_free, 1)
                dve.wait_ge(sc_free, h + 1)
                nc.vector.tensor_reduce(rowmax[:, h % 2, 1:2], pb[:, 0:T], AX_X, ALU.max)
                nc.vector.tensor_reduce(rowmax[:, h % 2, 0:1], pb[:, T:SQ], AX_X, ALU.max).then_inc(max_done, 1)
                dve.wait_ge(max_done, h + 1)
                nc.vector.tensor_scalar(negmax[:, h % 2, :], rowmax[:, h % 2, :], -1.0, None,
                                        ALU.mult).then_inc(neg_done, 1)

            def normalise(h):
                dve.wait_ge(exp_done, h + 1)
                halves = ((1, slice(0, T)), (0, slice(T, SQ)))
                pb = probs[:, h % 2, :]
                for half, cols in halves:
                    last = nc.vector.tensor_tensor_reduce(pb[:, cols], pb[:, cols], count[:, cols], 1.0, 0.0,
                                                          ALU.mult, ALU.add, den[:, h % 2, half:half + 1])
                last.then_inc(den_done, 1)
                dve.wait_ge(den_done, h + 1)
                nc.vector.reciprocal(rden[:, h % 2, :], den[:, h % 2, :]).then_inc(rden_done, 1)
                dve.wait_ge(rden_done, h + 1)
                for half, cols in halves:
                    last = nc.vector.tensor_scalar(pb[:, cols], pb[:, cols], rden[:, h % 2, half:half + 1], None,
                                                   ALU.mult)
                last.then_inc(p_ready, 1)

            def attn_lo(h):
                dve.wait_ge(ot_hi, h + 1)
                nc.vector.tensor_tensor(mixT_lo[:, h, :], ot[:, 0:T], mixT_hi[:, h, :].bitcast(F32),
                                        ALU.subtract).then_inc(ot_free, 1)

            def decay_scores(h):
                dve.wait_ge(sc_full, A_HEADS + h + 1)
                if h >= 2:
                    dve.wait_ge(ot_full, A_HEADS + h - 1)
                else:
                    dve.wait_ge(pT_full, A_HEADS)
                nc.vector.tensor_tensor(probs[:, h % 2, :], sc[:, 0:SQ], decay[:, h, :], ALU.mult).then_inc(sc_free, 1)

            def ret_meansq(h):
                dve.wait_ge(ret_sq, h + 1)
                nc.vector.tensor_scalar(rmean[:, h, :], rsum[:, h, :], 1.0 / R_DIM, EPS, ALU.mult,
                                        ALU.add).then_inc(ret_mean, 1)

            def ret_scale(h):
                dve.wait_ge(ret_rstd, h + 1)
                for half in range(HALVES):
                    last = nc.vector.tensor_scalar(retn[:, half, R_DIM * h:R_DIM * (h + 1)],
                                                   ot[:, R_DIM * half:R_DIM * (half + 1)],
                                                   rrstd[:, h, half:half + 1], None, ALU.mult)
                last.then_inc(ot_free, 1)

            def gate(g):
                dve.wait_ge(ot_free, A_HEADS + 2 * (g + 1))
                dve.wait_ge(tp_full, 2 * TB_GATED[g])
                for h in range(HALVES):
                    dve.wait_ge(acc_read[h], 12 + g + 1)
                    cols = slice(NB * g, NB * (g + 1))
                    nc.vector.tensor_tensor(stage[:, h, :], retn[:, h, cols], sgr[:, h, cols],
                                            ALU.mult).then_inc(gated, 1)

            def add_residual(parity, q, halves=range(HALVES)):
                for h in halves:
                    cols = xres[:, h, bass.ds(q * NB, NB)]
                    nc.vector.tensor_tensor(cols, acc[:, parity, h, :], cols, ALU.add).then_inc(acc_read[h], 1)

            def read_out_block(n):
                block_done(OUT0 + n)
                if n == 0:
                    dve.wait_ge(sq_done, 8)
                add_residual((OUT0 + n) % 2, n)

            def read_up(blk):
                block_done(blk)
                for h in range(HALVES):
                    dve.wait_ge(acc_read[h], blk)
                    nc.vector.scalar_tensor_tensor(stage[:, h, :], acc[:, 1, h, :], rstd[:, 1, h:h + 1],
                                                   stage[:, h, :], ALU.mult, ALU.mult).then_inc(acc_read[h], 1)

            def final_weights(q):
                dve.wait_ge(sq_done, q * 2 + 18)
                for h in range(HALVES):
                    cols = bass.ds(q * NB, NB)
                    last = nc.vector.tensor_tensor(xres[:, h, cols], xres[:, h, cols], wfin[:, cols], ALU.mult)
                    last.then_inc(z_done, 1)

            nc.vector.memset(junk[:, :], 0.0).then_inc(junk_ready, 1)
            dve.wait_ge(wcol_full, 1)
            nc.vector.tensor_copy(wcol[:, :], sc[:, 0:KT]).then_inc(wcol_ready, 1)
            nc.vector.tensor_copy(wcol2[:, :], sc[:, KT:2 * KT]).then_inc(wcol_ready, 1)
            dve.wait_ge(wcol_ready, 2)

            plan = Plan()
            plan.put(1, 2, lambda: mean_square(0, 8))
            plan.put(1, 3, query_scale)
            for b in range(IN_BLOCKS):
                plan.put(b + 1, 3, lambda b=b: read_in_block(b))
            for b, batch in TB_IN.items():
                s, n = IN_ORDER[b]
                if b == 8:
                    plan.put(b + 1, 6, lambda: dve.wait_ge(sc_full, A_HEADS))
                plan.put(b + 1, 6, lambda s=s, n=n, batch=batch: tiles_copy(qT if s in (QA, QR) else kT, 4 * n, batch))
            for h in range(A_HEADS):
                plan.put(0, ATTN_AT + 3 * h + 4, lambda h=h: mask_and_max(h))
                plan.put(0, ATTN_AT + 3 * h + 5, lambda h=h: normalise(h))
                plan.put(0, ATTN_AT + 3 * h + 10, lambda h=h: attn_lo(h))
            for h in range(R_HEADS):
                plan.put(0, RET_AT[h] + 4, lambda h=h: decay_scores(h))
                plan.put(0, RET_AT[h] + 7, lambda h=h: ret_meansq(h))
                plan.put(0, RET_AT[h] + 8, lambda h=h: ret_scale(h))
            for g in range(2):
                plan.put(13 + g, 4, lambda g=g: gate(g))
                plan.put(13 + g, 7, lambda g=g: tiles_lo(mixT_lo, mixT_hi, 8 + 4 * g, TB_GATED[g]))
            for n in range(OUT_BLOCKS):
                plan.put(OUT0 + n + 1, 3, lambda n=n: read_out_block(n))
                plan.put(OUT0 + n + 1, 6, lambda n=n: tiles_lo(xT_lo, xT_hi, 4 * n, TB_X2 + n, wcol2))
            plan.put(FFN0, 7, lambda: mean_square(1, 16))

            for b in range(FFN0 + 1):
                split(b, plan.of(b), {j: [lambda j=j: tiles_lo(xT_lo, xT_hi, 4 * (j // 2), j // 2, wcol, (j % 2,))]
                                      for j in range(PAIRS)} if b == 0 else None)
            dve.wait_ge(rstd_done, 2)
            split(FFN0 + 1, {})
            with dve.Fori(1, FFN_STEPS) as i:
                split(i * 2 + FFN0, {3: [lambda: read_up(i * 2 + (FFN0 - 1))],
                                     6: [lambda: tiles_lo(hT_lo, hT_hi, (i - 1) * 4, i + (TB_H - 1))]})
                split(i * 2 + (FFN0 + 1), {})

            def split_down(n, hooks):
                split_block(DPAIRS, n * DPAIRS + PAIRS * DOWN0, hooks)

            split_down(0, {3: [lambda: read_up(DOWN0 - 1)],
                           6: [lambda: tiles_lo(hT_lo, hT_hi, (FFN_STEPS - 1) * 4, TB_H + FFN_STEPS - 1)]})
            dve.wait_ge(wfin_in, 16)

            def read_down(n):
                dve.wait_ge(pair_used, n * DPAIRS + (PAIRS * DOWN0 + DPAIRS))
                add_residual(n, n)

            with dve.Fori(1, DOWN_BLOCKS - 1) as n:
                split_down(n, {2: [lambda: read_down(n - 1)], 7: [lambda: final_weights(n - 1)]})
            q = DOWN_BLOCKS - 2
            split_down(q + 1, {2: [lambda: (dve.wait_ge(pair_used, PAIRS * DOWN0 + DPAIRS * (q + 1)),
                                            add_residual(0, q))],
                               7: [lambda: final_weights(q)]})
            c3 = slice(3 * NB, 4 * NB)
            for h in range(HALVES):
                dve.wait_ge(last_full, h + 1)
                add_residual(1, 3, (h,))
                mean_square(2, 22 + h + 1, slice(h, h + 1), 2 + h)
                dve.wait_ge(rstd_done, 3 + h)
                r, c2 = rstd[:, 2, h:h + 1], xres[:, h, 2 * NB:3 * NB]
                if h == 0:
                    dve.wait_ge(z_done, 3 * HALVES)
                nc.vector.tensor_scalar(c2, c2, r, None, ALU.mult).then_inc(y_dve, 1)
                nc.vector.scalar_tensor_tensor(xres[:, h, c3], xres[:, h, c3], r, wfin[:, c3], ALU.mult,
                                               ALU.mult).then_inc(y_dve, 1)

        @block.gpsimd
        def _(pool):
            nc.gpsimd.memset(mhalf[:, :], -0.5).then_inc(mhalf_ready, 1)
            pool.wait_ge(mhalf_ready, 1)

            def rsqrt(norm, n, hs=slice(0, HALVES)):
                pool.wait_ge(mean_done, n + 1)
                nc.gpsimd.tensor_tensor(rstd[:, norm, hs], meansq[:, norm, hs], mhalf[:, hs],
                                        ALU.pow).then_inc(rstd_done, 1)

            rsqrt(0, 0)
            for h in range(R_HEADS):
                pool.wait_ge(ret_mean, h + 1)
                nc.gpsimd.tensor_tensor(rrstd[:, h, :], rmean[:, h, :], mhalf[:, :], ALU.pow).then_inc(ret_rstd, 1)
            rsqrt(1, 1)
            for h in range(HALVES):
                rsqrt(2, 2 + h, slice(h, h + 1))


_INS = ["x", "norm_mix_w", "w_in", "w_out", "norm_ffn_w", "w_gate", "w_up", "w_down", "norm_final_w"]


def _tables():
    import numpy as np

    p = np.arange(P)[:, None]
    gap = np.concatenate([P + p - np.arange(T)[None, :], p - np.arange(P)[None, :]], axis=1)
    count = sum(((gap >= 0) & (gap % d == 0) & (gap <= w)).astype(np.float32)
                for w, d in ((128, 1), (512, 4), (2048, 16)))
    dist = np.where(count > 0, -gap, -1e30).astype(np.float32)
    gap = np.concatenate([np.arange(T)[None, :] - p, np.arange(P)[None, :] - p], axis=1).astype(np.float64)
    log_gamma = np.log(1.0 - np.exp2(-5.0 - np.arange(R_HEADS)))
    decay = np.where(gap[:, None, :] >= 0, np.exp(log_gamma[None, :, None] * gap[:, None, :]), 0.0) / R_DIM ** 0.5
    slopes = [2.0 ** (-8.0 * (h + 1) / A_HEADS) for h in range(A_HEADS)]
    return np.eye(P, dtype=np.float32), dist, count.astype(np.float32), decay.astype(np.float32), slopes


def kernel(**inputs):
    import numpy as _np
    import concourse.bacc as _bacc
    from concourse import mybir as _mybir
    from concourse.bass_utils import run_bass_kernel_spmd as _run

    nc = _bacc.Bacc("TRN2", target_bir_lowering=False, num_devices=1)
    *tables, slopes = _tables()
    given = {name: inputs[name] for name in _INS}
    given.update(zip(("ident", "dist", "count", "decay"), tables))
    arrays, args = {}, []
    for name, a in given.items():
        a = _np.ascontiguousarray(a)
        arrays[f"in_{name}_dram"] = a
        args.append(nc.dram_tensor(f"in_{name}_dram", a.shape, _mybir.dt.from_np(a.dtype), kind="ExternalInput").ap())
    args.append(nc.dram_tensor("out_0_dram", (1, T, D), _mybir.dt.float32, kind="ExternalOutput").ap())
    build(nc, *args, slopes)
    r = _run(nc, [arrays], core_ids=[0])
    return r.results[0]["out_0_dram"]
```

```python
import concourse.bass as bass
from concourse import mybir
from contextlib import ExitStack

F32 = mybir.dt.float32
F32R = mybir.dt.float32r
ALU = mybir.AluOpType
ACT = mybir.ActivationFunctionType
AX_X = mybir.AxisListType.X

P = 128
T = 256
HALVES = T // P
D = 2048
NB = 512
KT = D // P
F = 5632
FKT = F // P
A_HEADS, A_DIM = 8, 128
R_HEADS, R_DIM = 4, 256
A_SCALE = float(A_DIM) ** -0.5
MIX = 1024
EPS = 1e-6
SQ = 384

QK_BLOCKS = 4
WARMING = 2
RAW = 4
RING = 4

IN_BLOCKS, OUT_BLOCKS, FFN_STEPS, DOWN_BLOCKS = 14, D // NB, F // NB, D // NB
PAIRS = KT // 2
DPAIRS = FKT // 2
CHUNKS, DCHUNKS = PAIRS // 2, DPAIRS // 2
OUT0 = IN_BLOCKS
FFN0 = OUT0 + OUT_BLOCKS
DOWN0 = FFN0 + 2 * FFN_STEPS

QA, KA, VA, QR, KR, VR, GR = range(7)
IN_ORDER = [(s, n) for s in (QA, KA, VA, VR, KR, QR, GR) for n in range(2)]

ATTN_AT, ATTN_STEP = 41, 3
RET_AT = (96, 99, 104, 107)

TB_IN = {b: 4 + i for i, b in enumerate(b for b, (s, _) in enumerate(IN_ORDER) if s in (QA, KA, KR, QR))}
TB_GATED = [4 + len(TB_IN), 5 + len(TB_IN)]
TB_X2 = TB_GATED[1] + 1
TB_H = TB_X2 + 4


def hi_banks(batch):
    return batch * 2 if isinstance(batch, int) and batch < 4 else batch * 2 - 2 * len(TB_IN)


def slot_uses(slot):
    return len(range(slot, DCHUNKS, RAW))


def slot_last_user(j, slots, per_block, first_block):
    if j >= slots or first_block or per_block % slots == 0:
        return slots
    last = max(k for k in range(per_block) if k % slots == j)
    return per_block + j - last


def build(nc, x, norm_mix_w, w_in, w_out, norm_ffn_w, w_gate, w_up, w_down, norm_final_w,
          ident_c, dist_c, count_c, decay_c, out, slopes):
    base = -(-nc.sbuf_base // 64) * 64

    def place(name, shape, dt, offset):
        return nc.alloc_sbuf_tensor_at(name, shape, dt, offset=base + offset)

    KB = 1024
    xT_hi = place("xT_hi", [P, KT, T], F32R, 0)
    xT_lo = place("xT_lo", [P, KT, T], F32R, 16 * KB)
    wfin = place("wfin", [P, D], F32, 0)
    xres = place("xres", [P, HALVES, D], F32, 32 * KB)
    region = 48 * KB
    hT_hi = place("hT_hi", [P, FKT, T], F32R, region)
    hT_lo = place("hT_lo", [P, FKT, T], F32R, region + 44 * KB)
    mixT_hi = place("mixT_hi", [P, KT, T], F32R, region)
    mixT_lo = place("mixT_lo", [P, KT, T], F32R, region + 16 * KB)
    qkT = place("qkT", [P, 2 * MIX // P, T], F32, region + 32 * KB)
    qT, kT = qkT[:, 0:MIX // P, :], qkT[:, MIX // P:, :]
    va = place("va", [P, HALVES, MIX], F32, region + 48 * KB)
    retn = place("retn", [P, HALVES, MIX], F32, region + 48 * KB)
    vr = place("vr", [P, HALVES, MIX], F32, region + 56 * KB)
    sgr = place("sgr", [P, HALVES, MIX], F32, region + 64 * KB)
    dist = place("dist", [P, SQ], F32, region + 72 * KB)
    count = place("count", [P, SQ], F32, region + 72 * KB + 1536)
    decay = place("decay", [P, R_HEADS, SQ], F32, region + 75 * KB)
    probs = place("probs", [P, 2, SQ], F32, region + 81 * KB)
    pT = place("pT", [P, 2, SQ], F32, region + 84 * KB)
    raw = place("raw", [P, RAW, 4, NB], F32, 136 * KB)
    w_hi = place("w_hi", [P, RING, 2, NB], F32R, 168 * KB)
    w_lo = place("w_lo", [P, RING, 2, NB], F32R, 184 * KB)
    stage = place("stage", [P, HALVES, NB], F32, 200 * KB)
    small_at = [204 * KB]

    def small(name, shape, dt=F32):
        n = 4
        for d in shape[1:]:
            n *= d
        offset = small_at[0]
        small_at[0] += -(-n // 32) * 32
        return place(name, shape, dt, offset)

    wrow = place("wrow", [KT, P], F32, 200 * KB)
    wrow2 = place("wrow2", [KT, P], F32, 200 * KB + 512)
    junk = small("junk", [P, NB])
    ident = small("ident", [P, P])
    wcol = small("wcol", [P, KT])
    wcol2 = small("wcol2", [P, KT])
    sumsq = small("sumsq", [P, 3, HALVES, 4])
    tot = small("tot", [P, 3, HALVES])
    meansq = small("meansq", [P, 3, HALVES])
    rstd = small("rstd", [P, 3, HALVES])
    mhalf = small("mhalf", [P, HALVES])
    rowmax = small("rowmax", [P, 2, HALVES])
    negmax = small("negmax", [P, 2, HALVES])
    den = small("den", [P, 2, HALVES])
    rden = small("rden", [P, 2, HALVES])
    rsum = small("rsum", [P, R_HEADS, HALVES])
    rmean = small("rmean", [P, R_HEADS, HALVES])
    rrstd = small("rrstd", [P, R_HEADS, HALVES])

    x_d = x.rearrange("b (h p) d -> (b p) h d", p=P)
    out_d = out.rearrange("b (h p) d -> (b p) h d", p=P)
    w_in_d = w_in.rearrange("l (k p) n -> (l p) k n", p=P)
    w_out_d = w_out.rearrange("l (k p) n -> (l p) k n", p=P)
    w_gate_d = w_gate.rearrange("l (k p) n -> (l p) k n", p=P)
    w_up_d = w_up.rearrange("l (k p) n -> (l p) k n", p=P)
    w_down_d = w_down.rearrange("l (k p) n -> (l p) k n", p=P)

    with ExitStack() as ctx:
        def sem(name):
            return ctx.enter_context(nc.semaphore(name))

        def bank(name, shape):
            return ctx.enter_context(nc.psum_tensor(name, shape, F32))

        acc = bank("acc", [P, 2, HALVES, NB])
        tp = bank("tp", [P, 2, 2, T])
        sc = bank("sc", [P, NB])
        ot = bank("ot", [P, NB])

        norm_in = sem("norm_in")
        const_in = sem("const_in")
        x_in = [sem(f"x_in{j}") for j in range(PAIRS)]
        wfin_in = sem("wfin_in")
        early_in = [sem(f"early_in{c}") for c in range(CHUNKS)]
        raw_in = [sem(f"raw_in{s}") for s in range(RAW)]
        hi_ready = sem("hi_ready")
        lo_ready = sem("lo_ready")
        pair_used = sem("pair_used")
        acc_read = [sem(f"acc_read{h}") for h in range(HALVES)]
        tp_full = sem("tp_full")
        tp_hi = sem("tp_hi")
        tp_free = sem("tp_free")
        junk_ready = sem("junk_ready")
        table_ready = sem("table_ready")
        warm = sem("warm")
        wcol_full = sem("wcol_full")
        wcol_ready = sem("wcol_ready")
        mhalf_ready = sem("mhalf_ready")
        sq_done = sem("sq_done")
        tot_done = sem("tot_done")
        mean_done = sem("mean_done")
        rstd_done = sem("rstd_done")
        sc_full = sem("sc_full")
        sc_free = sem("sc_free")
        max_done = sem("max_done")
        neg_done = sem("neg_done")
        exp_done = sem("exp_done")
        den_done = sem("den_done")
        rden_done = sem("rden_done")
        p_ready = sem("p_ready")
        pT_full = sem("pT_full")
        pT_ready = sem("pT_ready")
        ot_full = sem("ot_full")
        ot_hi = sem("ot_hi")
        ot_free = sem("ot_free")
        ret_sq = sem("ret_sq")
        ret_mean = sem("ret_mean")
        ret_rstd = sem("ret_rstd")
        gated = sem("gated")
        z_done = sem("z_done")
        last_full = sem("last_full")
        y_act = sem("y_act")
        y_dve = sem("y_dve")
        out_done = sem("out_done")

        tp_flat = tp[:, 0, :, :].rearrange("p a b -> p (a b)")
        block = ctx.enter_context(nc.Block())

        @block.sync
        def _(sp):
            sp.dma_start(ident[:, :], ident_c).then_inc(norm_in, 16)
            for j in range(PAIRS):
                cols = slice(2 * P * j, 2 * P * (j + 1))
                sp.dma_start(xres[:, :, cols], x_d[:, :, cols]).then_inc(x_in[j], 16)
                sp.dma_start(raw[:, j // 2, 2 * (j % 2):2 * (j % 2) + 2, :], w_in_d[:, 2 * j:2 * j + 2, 0:NB]
                             ).then_inc(raw_in[j // 2] if j % 2 else early_in[j // 2], 16)

            def load_block(w, col, blk):
                for c in range(CHUNKS):
                    sp.wait_ge(lo_ready, blk * PAIRS + (2 * c + 2 - PAIRS))
                    sp.dma_start(raw[:, c, :, :], w[:, 4 * c:4 * c + 4, bass.ds(col, NB)]).then_inc(raw_in[c], 16)

            with sp.Fori(1, 6) as b:
                load_block(w_in_d, b * NB, b)
            for b in range(6, IN_BLOCKS):
                s, n = IN_ORDER[b]
                load_block(w_in_d, MIX * s + NB * n, b)
            with sp.Fori(0, OUT_BLOCKS) as n:
                load_block(w_out_d, n * NB, n + OUT0)
            with sp.Fori(0, FFN_STEPS) as i:
                load_block(w_gate_d, i * NB, i * 2 + FFN0)
                load_block(w_up_d, i * NB, i * 2 + (FFN0 + 1))

            def load_down(n):
                for c in range(DCHUNKS):
                    back = slot_last_user(c, RAW, DCHUNKS, isinstance(n, int) and n == 0)
                    sp.wait_ge(lo_ready, n * DPAIRS + (PAIRS * DOWN0 + 2 * (c - back) + 2))
                    sp.dma_start(raw[:, c % RAW, :, :],
                                 w_down_d[:, 4 * c:4 * c + 4, bass.ds(n * NB, NB)]).then_inc(raw_in[c % RAW], 16)

            load_down(0)
            sp.wait_ge(pair_used, PAIRS * DOWN0)
            sp.dma_start(wfin[:, :], norm_final_w.partition_broadcast(P)).then_inc(wfin_in, 16)
            with sp.Fori(1, DOWN_BLOCKS) as n:
                load_down(n)
            for h in range(HALVES):
                for k in range(2):
                    for q, done in ((2 + k, y_dve), (k, y_act)):
                        sp.wait_ge(done, 2 * h + k + 1)
                        cols = slice(NB * q, NB * (q + 1))
                        sp.dma_start(out_d[:, h, cols], xres[:, h, cols]).then_inc(out_done, 16)
            sp.wait_ge(out_done, 16 * 4 * HALVES)

        @block.tensor
        def _(pe):
            def multiply_pair(a_hi, a_lo, pairs, parity, j, halves):
                for kk in range(2):
                    kt = 2 * j + kk
                    for h in halves:
                        hs = slice(P * h, P * (h + 1))
                        dst = acc[:, parity, h, :]
                        hi, lo = w_hi[:, j % RING, kk, :], w_lo[:, j % RING, kk, :]
                        nc.tensor.matmul(dst, a_hi[:, kt, hs], hi, start=(kt == 0), stop=False)
                        nc.tensor.matmul(dst, a_hi[:, kt, hs], lo, start=False, stop=False)
                        last = nc.tensor.matmul(dst, a_lo[:, kt, hs], hi, start=False, stop=(kt == 2 * pairs - 1))
                return last

            def multiply_block(a_hi, a_lo, pairs, before, blk, parity, between=None, inputs=None, last=False,
                               acc_known_free=False):
                if not acc_known_free and (not isinstance(blk, int) or blk >= 2):
                    for h in range(HALVES):
                        pe.wait_ge(acc_read[h], blk - 1)
                for j in range(pairs - RING if last else pairs):
                    if inputs:
                        inputs(j)
                    pe.wait_ge(lo_ready, before + (j + 1))
                    multiply_pair(a_hi, a_lo, pairs, parity, j, range(HALVES)).then_inc(pair_used, 1)
                    if between:
                        between(j)
                if last:
                    for h in range(HALVES):
                        for j in range(pairs - RING, pairs):
                            pe.wait_ge(lo_ready, before + (j + 1))
                            mm = multiply_pair(a_hi, a_lo, pairs, parity, j, (h,))
                        mm.then_inc(last_full, 1)

            def transpose_batch(src, batch, banks=range(2)):
                for b in banks:
                    if not isinstance(batch, int) or batch > 0:
                        pe.wait_ge(tp_free, batch * 2 + (b - 1))
                    for t in range(2):
                        for h in range(HALVES):
                            last = nc.tensor.transpose(tp[:, b, t, P * h:P * (h + 1)], src(2 * b + t, h), ident[:, :])
                    last.then_inc(tp_full, 1)

            def transpose_stage(batch):
                transpose_batch(lambda t, h: stage[:, h, P * t:P * (t + 1)], batch)

            def transpose_block(batch, blk):
                for h in range(HALVES):
                    pe.wait_ge(acc_read[h], blk + 1)
                transpose_stage(batch)

            def transpose_gated(g):
                pe.wait_ge(gated, HALVES * (g + 1))
                transpose_stage(TB_GATED[g])

            def transpose_residual(n):
                for h in range(HALVES):
                    pe.wait_ge(acc_read[h], OUT0 + n + 1)
                transpose_batch(lambda t, h: xres[:, h, NB * n + P * t:NB * n + P * (t + 1)], TB_X2 + n)

            def attn_scores(h):
                pe.wait_ge(tp_free, 2 * (TB_IN[2 + h // 4] + 1))
                if h > 0:
                    pe.wait_ge(sc_free, h)
                nc.tensor.matmul(sc[:, 0:T], qT[:, h, P:T], kT[:, h, :], start=True, stop=True)
                nc.tensor.matmul(sc[:, T:SQ], qT[:, h, 0:P], kT[:, h, 0:P], start=True, stop=True).then_inc(sc_full, 1)

            def attn_transpose(h):
                pe.wait_ge(p_ready, h + 1)
                if h > 0:
                    pe.wait_ge(pT_ready, h)
                pb = probs[:, h % 2, :]
                nc.tensor.transpose(tp_flat[:, 0:P], pb[:, T:SQ], ident[:, :])
                nc.tensor.transpose(tp_flat[:, P:T], pb[:, 0:P], ident[:, :])
                nc.tensor.transpose(tp_flat[:, T:SQ], pb[:, P:T], ident[:, :]).then_inc(pT_full, 1)

            def attn_out(h):
                pe.wait_ge(pT_ready, h + 1)
                for half in range(HALVES):
                    pe.wait_ge(acc_read[half], 4 + h // 4 + 1)
                if h > 0:
                    pe.wait_ge(ot_free, h)
                cols = slice(A_DIM * h, A_DIM * (h + 1))
                nc.tensor.matmul(ot[:, 0:T], va[:, 0, cols], pT[:, h % 2, 0:T], start=True, stop=False)
                nc.tensor.matmul(ot[:, P:T], va[:, 1, cols], pT[:, h % 2, T:SQ], start=False,
                                 stop=True).then_inc(ot_full, 1)

            def ret_scores(h):
                pe.wait_ge(tp_free, 2 * (TB_IN[10 + h // 2] + 1))
                pe.wait_ge(sc_free, A_HEADS + h)
                for dst, i0 in ((sc[:, 0:T], 0), (sc[:, T:SQ], P)):
                    for t in range(2):
                        last = nc.tensor.matmul(dst, kT[:, 2 * h + t, i0:i0 + P], qT[:, 2 * h + t, i0:T],
                                                start=(t == 0), stop=(t == 1))
                last.then_inc(sc_full, 1)

            def ret_out(h):
                pe.wait_ge(sc_free, A_HEADS + h + 1)
                for half in range(HALVES):
                    pe.wait_ge(acc_read[half], 6 + h // 2 + 1)
                pe.wait_ge(ot_free, A_HEADS + h)
                v, a = vr[:, :, R_DIM * h:R_DIM * (h + 1)], probs[:, h % 2, :]
                nc.tensor.matmul(ot[:, 0:R_DIM], a[:, 0:P], v[:, 0, :], start=True, stop=True)
                nc.tensor.matmul(ot[:, R_DIM:], a[:, P:T], v[:, 0, :], start=True, stop=False)
                nc.tensor.matmul(ot[:, R_DIM:], a[:, T:SQ], v[:, 1, :], start=False, stop=True).then_inc(ot_full, 1)

            pe.wait_ge(junk_ready, 1)
            for _ in range(WARMING):
                mm = nc.tensor.matmul(ot[:, :], junk[:, 0:P], junk[:, :], start=True, stop=True)
            mm.then_inc(warm, 1)
            pe.wait_ge(norm_in, 16 * 3)
            nc.tensor.transpose(sc[:, 0:KT], wrow[:, :], ident[0:KT, 0:KT])
            nc.tensor.transpose(sc[:, KT:2 * KT], wrow2[:, :], ident[0:KT, 0:KT]).then_inc(wcol_full, 1)

            def transpose_input(j):
                pe.wait_ge(x_in[j], 16)
                transpose_batch(lambda t, h: xres[:, h, NB * (j // 2) + P * t:NB * (j // 2) + P * (t + 1)],
                                j // 2, (j % 2,))

            for j in range(3):
                transpose_input(j)

            def between(b, j):
                s = PAIRS * b + j
                if b == 0 and j + 3 < PAIRS:
                    transpose_input(j + 3)
                if j == 2 and b - 1 in TB_IN:
                    if b - 1 == 8:
                        pe.wait_ge(pT_ready, A_HEADS)
                    transpose_block(TB_IN[b - 1], b - 1)
                for h in range(A_HEADS):
                    since = s - (ATTN_AT + ATTN_STEP * h)
                    if since == 0:
                        attn_scores(h)
                    if since == 4:
                        attn_transpose(h)
                    if since == 6:
                        attn_out(h)
                for h in range(R_HEADS):
                    if s == RET_AT[h]:
                        ret_scores(h)
                    if s == RET_AT[h] + 3:
                        ret_out(h)
                if j == 3 and b in (13, 14):
                    transpose_gated(b - 13)
                if j == 2 and b > OUT0:
                    transpose_residual(b - 1 - OUT0)

            def tiles_ready(batch):
                pe.wait_ge(tp_free, 2 * (batch + 1))

            def width_block(b, parity, a_hi=xT_hi, a_lo=xT_lo, between=None, inputs=None, acc_known_free=False):
                multiply_block(a_hi, a_lo, PAIRS, b * PAIRS, b, parity, between, inputs,
                               acc_known_free=acc_known_free)

            width_block(0, 0, between=lambda j: between(0, j), inputs=lambda j: pe.wait_ge(tp_free, j + 1))
            with pe.Fori(0, 2) as s:
                for n in range(2):
                    def transpose_qk(j, s=s, n=n):
                        if j == 2:
                            transpose_block(s * 2 + (TB_IN[0] + n), s * 2 + n)
                    width_block(s * 2 + (n + 1), 1 - n, between=transpose_qk, acc_known_free=True)
            for b in range(QK_BLOCKS + 1, IN_BLOCKS):
                width_block(b, b % 2, between=lambda j: between(b, j))

            def mixed_ready(j):
                if j == 0:
                    pe.wait_ge(ot_free, A_HEADS)
                if j in (4, 6):
                    tiles_ready(TB_GATED[j // 2 - 2])

            for b in range(OUT0, FFN0):
                width_block(b, b % 2, mixT_hi, mixT_lo, lambda j: between(b, j), mixed_ready if b == OUT0 else None)

            def residual_ready(j):
                if j % 2 == 0:
                    tiles_ready(TB_X2 + j // 2)

            width_block(FFN0, 0, between=lambda j: between(FFN0, j), inputs=residual_ready)
            width_block(FFN0 + 1, 1)
            with pe.Fori(1, FFN_STEPS) as i:
                def transpose_hidden(j):
                    if j == 2:
                        transpose_block(i + (TB_H - 1), i * 2 + (FFN0 - 1))
                width_block(i * 2 + FFN0, 0, between=transpose_hidden)
                width_block(i * 2 + (FFN0 + 1), 1)

            def down_block(n, parity, between=None, inputs=None, last=False):
                multiply_block(hT_hi, hT_lo, DPAIRS, n * DPAIRS + PAIRS * DOWN0, n + DOWN0, parity,
                               between, inputs, last)

            def transpose_last_hidden(j):
                if j == 2:
                    transpose_block(TB_H + FFN_STEPS - 1, DOWN0 - 1)

            def hidden_ready(j):
                if j == 0:
                    tiles_ready(TB_H + FFN_STEPS - 2)
                if j == 2 * (FFN_STEPS - 1):
                    tiles_ready(TB_H + FFN_STEPS - 1)

            down_block(0, 0, transpose_last_hidden, hidden_ready)
            with pe.Fori(1, DOWN_BLOCKS - 1) as n:
                down_block(n, n * -1 + 2)
            down_block(DOWN_BLOCKS - 1, 1, last=True)

        @block.scalar
        def _(act):
            act.dma_start(wrow[:, :], norm_mix_w.rearrange("l (k p) -> (l k) p", p=P)).then_inc(norm_in, 16)
            act.dma_start(wrow2[:, :], norm_ffn_w.rearrange("l (k p) -> (l k) p", p=P)).then_inc(norm_in, 16)

            act.wait_ge(junk_ready, 1)
            nc.scalar.activation(sumsq[:, 0, 0, 0:1], junk[:, 0:1], ACT.Copy).then_inc(table_ready, 1)

            def load_tables():
                act.dma_start(dist[:, :], dist_c).then_inc(const_in, 16)
                act.dma_start(count[:, :], count_c).then_inc(const_in, 16)
                act.dma_start(decay[:, :, :], decay_c).then_inc(const_in, 16)

            def split_block(pairs, before, landed, between=None):
                for j in range(pairs):
                    landed(j)
                    back = slot_last_user(j, RING, pairs, isinstance(before, int) and before <= PAIRS * DOWN0)
                    if not isinstance(before, int) or before + j >= back:
                        act.wait_ge(pair_used, before + (j - back + 1))
                    nc.scalar.activation(w_hi[:, j % RING, :, :],
                                         raw[:, (j // 2) % RAW, 2 * (j % 2):2 * (j % 2) + 2, :],
                                         ACT.Copy).then_inc(hi_ready, 1)
                    if between:
                        between(j)

            def split(blk, between=None):
                def landed(j):
                    if j % 2 == 0:
                        act.wait_ge(raw_in[j // 2], blk * 16 + 16)
                split_block(PAIRS, blk * PAIRS, landed, between)

            def tiles_hi(dst, kt0, batch, w=None, banks=range(2)):
                for b in banks:
                    act.wait_ge(tp_full, batch * 2 + (b + 1))
                    if w is None:
                        nc.scalar.activation(dst[:, bass.ds(kt0 + 2 * b, 2), :], tp[:, b, :, :],
                                             ACT.Copy).then_inc(tp_hi, 1)
                    else:
                        for t in range(2):
                            kt = kt0 + 2 * b + t
                            last = nc.scalar.activation(dst[:, kt, :], tp[:, b, t, :], ACT.Copy,
                                                        scale=w[:, kt:kt + 1])
                        last.then_inc(tp_hi, 1)

            def square(norm, h, q):
                if isinstance(q, int) and norm + q + h == 0:
                    act.wait_ge(warm, 1)
                    act.wait_ge(table_ready, 1)
                else:
                    act.wait_ge(sq_done, q * 2 + (8 * norm + h))
                if norm == 1 and q + h == 0:
                    act.wait_ge(ret_sq, R_HEADS)
                nc.scalar.activation(junk[:, :], xres[:, h, bass.ds(q * NB, NB)], ACT.Square,
                                     accum_out=sumsq[:, norm, h, bass.ds(q, 1)]).then_inc(sq_done, 1)

            def block_done(blk):
                act.wait_ge(pair_used, (blk + 1) * PAIRS)

            def read_in_block(b):
                s, n = IN_ORDER[b]
                block_done(b)
                src, cols = acc[:, b % 2, :, :], slice(NB * n, NB * (n + 1))
                if s == GR:
                    for h in range(HALVES):
                        nc.scalar.activation(sgr[:, h, cols], src[:, h, :], ACT.Silu,
                                             scale=rstd[:, 0, h:h + 1]).then_inc(acc_read[h], 1)
                elif s in (VA, VR):
                    dst = va if s == VA else vr
                    nc.scalar.activation(dst[:, 0, cols], src[:, 0, :], ACT.Copy,
                                         scale=rstd[:, 0, 0:1]).then_inc(acc_read[0], 1)
                else:
                    act.wait_ge(tp_full, 2 * TB_IN[b])
                    nc.scalar.activation(stage[:, 0, :], src[:, 0, :], ACT.Copy,
                                         scale=rstd[:, 0, 0:1]).then_inc(acc_read[0], 1)

            def read_qk_block(s, n):
                block_done(s * 2 + n)
                act.wait_ge(tp_full, s * 4 + 2 * (TB_IN[0] + n))
                act.wait_ge(rstd_done, 1)
                nc.scalar.activation(stage[:, 0, :], acc[:, n, 0, :], ACT.Copy,
                                     scale=rstd[:, 0, 0:1]).then_inc(acc_read[0], 1)

            def exps(h):
                act.wait_ge(neg_done, h + 1)
                for half, cols in ((1, slice(0, T)), (0, slice(T, SQ))):
                    last = nc.scalar.activation(probs[:, h % 2, cols], probs[:, h % 2, cols], ACT.Exp,
                                                bias=negmax[:, h % 2, half:half + 1], scale=A_SCALE)
                last.then_inc(exp_done, 1)

            def copy_pT(h):
                act.wait_ge(pT_full, h + 1)
                if h >= 2:
                    act.wait_ge(ot_full, h - 1)
                nc.scalar.activation(pT[:, h % 2, :], tp_flat[:, 0:SQ], ACT.Copy).then_inc(pT_ready, 1)

            def attn_hi(h):
                act.wait_ge(ot_full, h + 1)
                nc.scalar.activation(mixT_hi[:, h, :], ot[:, 0:T], ACT.Copy).then_inc(ot_hi, 1)

            def ret_squares(h):
                act.wait_ge(ot_full, A_HEADS + h + 1)
                if h > 0:
                    act.wait_ge(ret_sq, h)
                else:
                    act.wait_ge(sq_done, 8)
                for half in range(HALVES):
                    cols = slice(R_DIM * half, R_DIM * (half + 1))
                    last = nc.scalar.activation(junk[:, cols], ot[:, cols], ACT.Square,
                                                accum_out=rsum[:, h, half:half + 1])
                last.then_inc(ret_sq, 1)

            def residual_squares(norm, q, blk):
                for h in range(HALVES):
                    act.wait_ge(acc_read[h], blk + 1)
                    square(norm, h, q)

            def read_gate(i, blk):
                block_done(blk)
                act.wait_ge(tp_full, (i + TB_H) * 2)
                for h in range(HALVES):
                    nc.scalar.activation(stage[:, h, :], acc[:, 0, h, :], ACT.Silu,
                                         scale=rstd[:, 1, h:h + 1]).then_inc(acc_read[h], 1)

            def input_hi(j):
                tiles_hi(xT_hi, 4 * (j // 2), j // 2, wcol, (j % 2,))

            def landed_early(j):
                act.wait_ge(raw_in[j // 2] if j % 2 else early_in[j // 2], 16)

            def between(b, j):
                s = PAIRS * b + j
                if b == 0:
                    if j + 1 < PAIRS:
                        input_hi(j + 1)
                    if j == 5:
                        load_tables()
                    if j > 0:
                        square(0, (j - 1) % 2, (j - 1) // 2)
                if j == 3 and QK_BLOCKS <= b - 1 < IN_BLOCKS:
                    read_in_block(b - 1)
                if j == 4 and b > OUT0:
                    residual_squares(1, b - 1 - OUT0, b - 1)
                if j == 6 and b > OUT0:
                    tiles_hi(xT_hi, 4 * (b - 1 - OUT0), TB_X2 + b - 1 - OUT0, wcol2)
                for h in range(A_HEADS):
                    since = s - (ATTN_AT + ATTN_STEP * h)
                    if since == 4:
                        exps(h)
                    if since == 8:
                        copy_pT(h)
                    if since == 10:
                        attn_hi(h)
                for h in range(R_HEADS):
                    if s == RET_AT[h] + 7:
                        ret_squares(h)
                if j == 7 and b in (13, 14):
                    tiles_hi(mixT_hi, 8 + 4 * (b - 13), TB_GATED[b - 13])

            act.wait_ge(wcol_ready, 2)
            input_hi(0)
            split_block(PAIRS, 0, landed_early, lambda j: between(0, j))
            square(0, 1, 3)
            with act.Fori(0, 2) as s:
                for n in range(2):
                    split(s * 2 + (n + 1), lambda j: read_qk_block(s, n) if j == 3 else None)
            for b in range(QK_BLOCKS + 1, FFN0 + 1):
                split(b, lambda j: between(b, j))
            act.wait_ge(rstd_done, 2)
            split(FFN0 + 1, lambda j: read_gate(0, FFN0) if j == 3 else None)
            with act.Fori(1, FFN_STEPS) as i:
                def hidden_hi(j):
                    if j == 6:
                        tiles_hi(hT_hi, (i - 1) * 4, i + (TB_H - 1))

                def gate(j):
                    if j == 3:
                        read_gate(i, i * 2 + FFN0)
                split(i * 2 + FFN0, hidden_hi)
                split(i * 2 + (FFN0 + 1), gate)

            def split_down(n, between):
                def landed(j):
                    slot, use = j // 2 % RAW, j // 2 // RAW
                    if j % 2 == 0:
                        act.wait_ge(raw_in[slot], n * (16 * slot_uses(slot)) + 16 * (DOWN0 + use + 1))

                split_block(DPAIRS, n * DPAIRS + PAIRS * DOWN0, landed, between)

            def last_hidden_hi(j):
                if j == 6:
                    tiles_hi(hT_hi, (FFN_STEPS - 1) * 4, TB_H + FFN_STEPS - 1)

            split_down(0, last_hidden_hi)
            with act.Fori(1, DOWN_BLOCKS) as n:
                def down_squares(j):
                    if j == 3:
                        residual_squares(2, n - 1, n + (DOWN0 - 1))
                split_down(n, down_squares)
            for h in range(HALVES):
                act.wait_ge(acc_read[h], DOWN0 + DOWN_BLOCKS)
                square(2, h, DOWN_BLOCKS - 1)
                act.wait_ge(rstd_done, 3 + h)
                act.wait_ge(z_done, 2 * HALVES)
                for q in range(2):
                    cols = xres[:, h, NB * q:NB * (q + 1)]
                    nc.scalar.activation(cols, cols, ACT.Copy, scale=rstd[:, 2, h:h + 1]).then_inc(y_act, 1)

        @block.vector
        def _(dve):
            def split_block(pairs, before, between=None):
                for j in range(pairs):
                    dve.wait_ge(hi_ready, before + (j + 1))
                    nc.vector.tensor_tensor(w_lo[:, j % RING, :, :],
                                            raw[:, (j // 2) % RAW, 2 * (j % 2):2 * (j % 2) + 2, :],
                                            w_hi[:, j % RING, :, :].bitcast(F32), ALU.subtract).then_inc(lo_ready, 1)
                    if between:
                        between(j)

            def split(blk, between=None):
                split_block(PAIRS, blk * PAIRS, between)

            def tiles_lo(dst, src_hi, kt0, batch, w=None, banks=range(2)):
                for b in banks:
                    dve.wait_ge(tp_hi, hi_banks(batch) + (b + 1))
                    if w is None:
                        kts = bass.ds(kt0 + 2 * b, 2)
                        nc.vector.tensor_tensor(dst[:, kts, :], tp[:, b, :, :], src_hi[:, kts, :].bitcast(F32),
                                                ALU.subtract).then_inc(tp_free, 1)
                    else:
                        for t in range(2):
                            kt = kt0 + 2 * b + t
                            last = nc.vector.scalar_tensor_tensor(dst[:, kt, :], tp[:, b, t, :], w[:, kt:kt + 1],
                                                                  src_hi[:, kt, :].bitcast(F32),
                                                                  ALU.mult, ALU.subtract)
                        last.then_inc(tp_free, 1)

            def tiles_copy(dst, kt0, batch):
                for b in range(2):
                    dve.wait_ge(tp_full, batch * 2 + (b + 1))
                    nc.vector.tensor_copy(dst[:, bass.ds(kt0 + 2 * b, 2), :], tp[:, b, :, :]).then_inc(tp_free, 1)

            def block_done(blk):
                dve.wait_ge(pair_used, (blk + 1) * PAIRS)

            def read_in_block(b):
                s, n = IN_ORDER[b]
                if s == GR:
                    return
                block_done(b)
                src, r = acc[:, b % 2, 1, :], rstd[:, 0, 1:2]
                if s in (VA, VR):
                    dst = (va if s == VA else vr)[:, 1, NB * n:NB * (n + 1)]
                else:
                    dve.wait_ge(tp_full, 2 * TB_IN[b])
                    dst = stage[:, 1, :]
                nc.vector.tensor_scalar(dst, src, r, None, ALU.mult).then_inc(acc_read[1], 1)

            def read_qk_block(s, n):
                block_done(s * 2 + n)
                dve.wait_ge(tp_full, s * 4 + 2 * (TB_IN[0] + n))
                dve.wait_ge(rstd_done, 1)
                nc.vector.tensor_scalar(stage[:, 1, :], acc[:, n, 1, :], rstd[:, 0, 1:2], None,
                                        ALU.mult).then_inc(acc_read[1], 1)

            def mean_square(norm, n_squares, hs=slice(0, HALVES), n=None):
                n = norm if n is None else n
                dve.wait_ge(sq_done, n_squares)
                nc.vector.tensor_reduce(tot[:, norm, hs], sumsq[:, norm, hs, :], AX_X, ALU.add).then_inc(tot_done, 1)
                dve.wait_ge(tot_done, n + 1)
                nc.vector.tensor_scalar(meansq[:, norm, hs], tot[:, norm, hs], 1.0 / D, EPS, ALU.mult,
                                        ALU.add).then_inc(mean_done, 1)

            def mask_and_max(h):
                if h == 0:
                    dve.wait_ge(const_in, 16 * 3)
                dve.wait_ge(sc_full, h + 1)
                if h >= 2:
                    dve.wait_ge(pT_full, h - 1)
                pb = probs[:, h % 2, :]
                nc.vector.scalar_tensor_tensor(pb, dist[:, :], slopes[h] / A_SCALE, sc[:, 0:SQ], ALU.mult,
                                               ALU.add).then_inc(sc_free, 1)
                dve.wait_ge(sc_free, h + 1)
                nc.vector.tensor_reduce(rowmax[:, h % 2, 1:2], pb[:, 0:T], AX_X, ALU.max)
                nc.vector.tensor_reduce(rowmax[:, h % 2, 0:1], pb[:, T:SQ], AX_X, ALU.max).then_inc(max_done, 1)
                dve.wait_ge(max_done, h + 1)
                nc.vector.tensor_scalar(negmax[:, h % 2, :], rowmax[:, h % 2, :], -A_SCALE, None,
                                        ALU.mult).then_inc(neg_done, 1)

            def normalise(h):
                dve.wait_ge(exp_done, h + 1)
                halves = ((1, slice(0, T)), (0, slice(T, SQ)))
                pb = probs[:, h % 2, :]
                for half, cols in halves:
                    last = nc.vector.tensor_tensor_reduce(pb[:, cols], pb[:, cols], count[:, cols], 1.0, 0.0,
                                                          ALU.mult, ALU.add, den[:, h % 2, half:half + 1])
                last.then_inc(den_done, 1)
                dve.wait_ge(den_done, h + 1)
                nc.vector.reciprocal(rden[:, h % 2, :], den[:, h % 2, :]).then_inc(rden_done, 1)
                dve.wait_ge(rden_done, h + 1)
                for half, cols in halves:
                    last = nc.vector.tensor_scalar(pb[:, cols], pb[:, cols], rden[:, h % 2, half:half + 1], None,
                                                   ALU.mult)
                last.then_inc(p_ready, 1)

            def attn_lo(h):
                dve.wait_ge(ot_hi, h + 1)
                nc.vector.tensor_tensor(mixT_lo[:, h, :], ot[:, 0:T], mixT_hi[:, h, :].bitcast(F32),
                                        ALU.subtract).then_inc(ot_free, 1)

            def decay_scores(h):
                dve.wait_ge(sc_full, A_HEADS + h + 1)
                if h >= 2:
                    dve.wait_ge(ot_full, A_HEADS + h - 1)
                else:
                    dve.wait_ge(pT_full, A_HEADS)
                nc.vector.tensor_tensor(probs[:, h % 2, :], sc[:, 0:SQ], decay[:, h, :], ALU.mult).then_inc(sc_free, 1)

            def ret_meansq(h):
                dve.wait_ge(ret_sq, h + 1)
                nc.vector.tensor_scalar(rmean[:, h, :], rsum[:, h, :], 1.0 / R_DIM, EPS, ALU.mult,
                                        ALU.add).then_inc(ret_mean, 1)

            def ret_scale(h):
                dve.wait_ge(ret_rstd, h + 1)
                for half in range(HALVES):
                    last = nc.vector.tensor_scalar(retn[:, half, R_DIM * h:R_DIM * (h + 1)],
                                                   ot[:, R_DIM * half:R_DIM * (half + 1)],
                                                   rrstd[:, h, half:half + 1], None, ALU.mult)
                last.then_inc(ot_free, 1)

            def gate(g):
                dve.wait_ge(ot_free, A_HEADS + 2 * (g + 1))
                dve.wait_ge(tp_full, 2 * TB_GATED[g])
                for h in range(HALVES):
                    dve.wait_ge(acc_read[h], 12 + g + 1)
                    cols = slice(NB * g, NB * (g + 1))
                    nc.vector.tensor_tensor(stage[:, h, :], retn[:, h, cols], sgr[:, h, cols],
                                            ALU.mult).then_inc(gated, 1)

            def add_residual(parity, q, halves=range(HALVES)):
                for h in halves:
                    cols = xres[:, h, bass.ds(q * NB, NB)]
                    nc.vector.tensor_tensor(cols, acc[:, parity, h, :], cols, ALU.add).then_inc(acc_read[h], 1)

            def read_out_block(n):
                block_done(OUT0 + n)
                if n == 0:
                    dve.wait_ge(sq_done, 8)
                add_residual((OUT0 + n) % 2, n)

            def read_up(blk):
                block_done(blk)
                for h in range(HALVES):
                    dve.wait_ge(acc_read[h], blk)
                    nc.vector.scalar_tensor_tensor(stage[:, h, :], acc[:, 1, h, :], rstd[:, 1, h:h + 1],
                                                   stage[:, h, :], ALU.mult, ALU.mult).then_inc(acc_read[h], 1)

            def final_weights(q):
                dve.wait_ge(sq_done, q * 2 + 18)
                for h in range(HALVES):
                    cols = bass.ds(q * NB, NB)
                    last = nc.vector.tensor_tensor(xres[:, h, cols], xres[:, h, cols], wfin[:, cols], ALU.mult)
                    last.then_inc(z_done, 1)

            nc.vector.memset(junk[:, :], 0.0).then_inc(junk_ready, 1)
            dve.wait_ge(wcol_full, 1)
            nc.vector.tensor_copy(wcol[:, :], sc[:, 0:KT]).then_inc(wcol_ready, 1)
            nc.vector.tensor_copy(wcol2[:, :], sc[:, KT:2 * KT]).then_inc(wcol_ready, 1)
            dve.wait_ge(wcol_ready, 2)

            def input_lo(j):
                tiles_lo(xT_lo, xT_hi, 4 * (j // 2), j // 2, wcol, (j % 2,))

            def between(b, j):
                s = PAIRS * b + j
                if b == 0 and j + 1 < PAIRS:
                    input_lo(j + 1)
                if j == 3 and QK_BLOCKS <= b - 1 < IN_BLOCKS:
                    read_in_block(b - 1)
                if j == 3 and b > OUT0:
                    read_out_block(b - 1 - OUT0)
                if j == 6 and QK_BLOCKS <= b - 1 and b - 1 in TB_IN:
                    part, n = IN_ORDER[b - 1]
                    if b - 1 == 8:
                        dve.wait_ge(sc_full, A_HEADS)
                    tiles_copy(qT if part == QR else kT, 4 * n, TB_IN[b - 1])
                if j == 6 and b > OUT0:
                    tiles_lo(xT_lo, xT_hi, 4 * (b - 1 - OUT0), TB_X2 + b - 1 - OUT0, wcol2)
                if j == 7 and b == FFN0:
                    mean_square(1, 16)
                for h in range(A_HEADS):
                    since = s - (ATTN_AT + ATTN_STEP * h)
                    if since == 4:
                        mask_and_max(h)
                    if since == 5:
                        normalise(h)
                    if since == 10:
                        attn_lo(h)
                for h in range(R_HEADS):
                    since = s - RET_AT[h]
                    if since == 4:
                        decay_scores(h)
                    if since == 7:
                        ret_meansq(h)
                    if since == 8:
                        ret_scale(h)
                if j == 4 and b in (13, 14):
                    gate(b - 13)
                if j == 7 and b in (13, 14):
                    tiles_lo(mixT_lo, mixT_hi, 8 + 4 * (b - 13), TB_GATED[b - 13])

            input_lo(0)
            split_block(PAIRS, 0, lambda j: between(0, j))
            mean_square(0, 8)
            with dve.Fori(0, 2) as s:
                for n in range(2):
                    def qk_block(j, s=s, n=n):
                        if j == 3:
                            read_qk_block(s, n)
                        if j == 6:
                            tiles_copy(qkT, s * (MIX // P) + 4 * n, s * 2 + (TB_IN[0] + n))
                    split(s * 2 + (n + 1), qk_block)
            for b in range(QK_BLOCKS + 1, FFN0 + 1):
                split(b, lambda j: between(b, j))
            dve.wait_ge(rstd_done, 2)
            split(FFN0 + 1)
            with dve.Fori(1, FFN_STEPS) as i:
                def hidden(j):
                    if j == 3:
                        read_up(i * 2 + (FFN0 - 1))
                    if j == 6:
                        tiles_lo(hT_lo, hT_hi, (i - 1) * 4, i + (TB_H - 1))
                split(i * 2 + FFN0, hidden)
                split(i * 2 + (FFN0 + 1))

            def split_down(n, between):
                split_block(DPAIRS, n * DPAIRS + PAIRS * DOWN0, between)

            def last_hidden(j):
                if j == 3:
                    read_up(DOWN0 - 1)
                if j == 6:
                    tiles_lo(hT_lo, hT_hi, (FFN_STEPS - 1) * 4, TB_H + FFN_STEPS - 1)

            def read_down(n, parity, j):
                if j == 2:
                    dve.wait_ge(pair_used, n * DPAIRS + (PAIRS * DOWN0 + DPAIRS))
                    add_residual(parity, n)
                if j == 7:
                    final_weights(n)

            split_down(0, last_hidden)
            dve.wait_ge(wfin_in, 16)
            with dve.Fori(1, DOWN_BLOCKS - 1) as n:
                split_down(n, lambda j: read_down(n - 1, n - 1, j))
            split_down(DOWN_BLOCKS - 1, lambda j: read_down(DOWN_BLOCKS - 2, 0, j))
            c3 = slice(3 * NB, 4 * NB)
            for h in range(HALVES):
                dve.wait_ge(last_full, h + 1)
                add_residual(1, 3, (h,))
                mean_square(2, 22 + h + 1, slice(h, h + 1), 2 + h)
                dve.wait_ge(rstd_done, 3 + h)
                r, c2 = rstd[:, 2, h:h + 1], xres[:, h, 2 * NB:3 * NB]
                if h == 0:
                    dve.wait_ge(z_done, 3 * HALVES)
                nc.vector.tensor_scalar(c2, c2, r, None, ALU.mult).then_inc(y_dve, 1)
                nc.vector.scalar_tensor_tensor(xres[:, h, c3], xres[:, h, c3], r, wfin[:, c3], ALU.mult,
                                               ALU.mult).then_inc(y_dve, 1)

        @block.gpsimd
        def _(pool):
            nc.gpsimd.memset(mhalf[:, :], -0.5).then_inc(mhalf_ready, 1)
            pool.wait_ge(mhalf_ready, 1)

            def rsqrt(norm, n, hs=slice(0, HALVES)):
                pool.wait_ge(mean_done, n + 1)
                nc.gpsimd.tensor_tensor(rstd[:, norm, hs], meansq[:, norm, hs], mhalf[:, hs],
                                        ALU.pow).then_inc(rstd_done, 1)

            rsqrt(0, 0)
            for h in range(R_HEADS):
                pool.wait_ge(ret_mean, h + 1)
                nc.gpsimd.tensor_tensor(rrstd[:, h, :], rmean[:, h, :], mhalf[:, :], ALU.pow).then_inc(ret_rstd, 1)
            rsqrt(1, 1)
            for h in range(HALVES):
                rsqrt(2, 2 + h, slice(h, h + 1))


_INS = ["x", "norm_mix_w", "w_in", "w_out", "norm_ffn_w", "w_gate", "w_up", "w_down", "norm_final_w"]


def _tables():
    import numpy as np

    p = np.arange(P)[:, None]
    gap = np.concatenate([P + p - np.arange(T)[None, :], p - np.arange(P)[None, :]], axis=1)
    count = sum(((gap >= 0) & (gap % d == 0) & (gap <= w)).astype(np.float32)
                for w, d in ((128, 1), (512, 4), (2048, 16)))
    dist = np.where(count > 0, -gap, -1e30).astype(np.float32)
    gap = np.concatenate([np.arange(T)[None, :] - p, np.arange(P)[None, :] - p], axis=1).astype(np.float64)
    log_gamma = np.log(1.0 - np.exp2(-5.0 - np.arange(R_HEADS)))
    decay = np.where(gap[:, None, :] >= 0, np.exp(log_gamma[None, :, None] * gap[:, None, :]), 0.0) / R_DIM ** 0.5
    slopes = [2.0 ** (-8.0 * (h + 1) / A_HEADS) for h in range(A_HEADS)]
    return np.eye(P, dtype=np.float32), dist, count.astype(np.float32), decay.astype(np.float32), slopes


def kernel(**inputs):
    import numpy as _np
    import concourse.bacc as _bacc
    from concourse import mybir as _mybir
    from concourse.bass_utils import run_bass_kernel_spmd as _run

    nc = _bacc.Bacc("TRN2", target_bir_lowering=False, num_devices=1)
    *tables, slopes = _tables()
    given = {name: inputs[name] for name in _INS}
    given.update(zip(("ident", "dist", "count", "decay"), tables))
    arrays, args = {}, []
    for name, a in given.items():
        a = _np.ascontiguousarray(a)
        arrays[f"in_{name}_dram"] = a
        args.append(nc.dram_tensor(f"in_{name}_dram", a.shape, _mybir.dt.from_np(a.dtype), kind="ExternalInput").ap())
    args.append(nc.dram_tensor("out_0_dram", (1, T, D), _mybir.dt.float32, kind="ExternalOutput").ap())
    build(nc, *args, slopes)
    r = _run(nc, [arrays], core_ids=[0])
    return r.results[0]["out_0_dram"]
```
